# Optimizing a Trainium2 kernel written in Bass

```python
import jax
import jax.numpy as jnp
from jax import lax
import numpy as np

D_MODEL = 1024
BATCH = 1
SEQ = 512
DEPTH = 1

GRID_W = 64
CTX_LEN = 256
RET_HEADS = 4
RET_W = D_MODEL // 2
RET_HEAD_DIM = RET_W // RET_HEADS
MLSTM_HEADS = 4
MLSTM_W = D_MODEL // 2
MLSTM_HEAD_DIM = MLSTM_W // MLSTM_HEADS
MIX_W = RET_W + MLSTM_W
GATE_COLS = 4 * MLSTM_HEADS
IN_COLS = 4 * RET_W + 4 * MLSTM_W + GATE_COLS
CONV_W = 3
CHUNK = 128
ROPE_BASE = 10000.0
N_EXPERTS = 64
TOP_K = 8
N_GROUPS = 8
TOPK_GROUPS = 4
EXPERT_FF = 256
SHARED_FF = 256
ROUTED_SCALE = 2.5
EXPERT_BLOCK = 128
N_MOD = 6
EPS = 1e-6

kernel_name = 'hybrid_retention_mlstm_moe_dit_block'

def rmsnorm(x, g):
    x32 = x.astype(jnp.float32)
    y = x32 * lax.rsqrt(jnp.mean(x32 * x32, axis=-1, keepdims=True) + EPS)
    return (y * g.astype(jnp.float32)).astype(x.dtype)

def modulate(h, shift, scale):
    return h * (1.0 + scale) + shift

def head_norm(t, gain):
    t32 = t.astype(jnp.float32)
    mu = jnp.mean(t32, axis=-1, keepdims=True)
    var = jnp.mean(jnp.square(t32 - mu), axis=-1, keepdims=True)
    y = (t32 - mu) * lax.rsqrt(var + EPS)
    B, H, N, Dh = t.shape
    return y.transpose(0, 2, 1, 3).reshape(B, N, H * Dh) * gain.astype(jnp.float32)

def split_heads(t, n_heads):
    B, N, W = t.shape
    return t.reshape(B, N, n_heads, W // n_heads).transpose(0, 2, 1, 3)

def flip_seq(t):
    return None if t is None else jnp.flip(t, axis=2)

def to_chunks(t):
    B, H, N = t.shape[:3]
    return jnp.moveaxis(t.reshape(B, H, N // CHUNK, CHUNK, *t.shape[3:]), 2, 0)

def from_chunks(t):
    t = jnp.moveaxis(t, 0, 2)
    B, H, nc, C = t.shape[:4]
    return t.reshape(B, H, nc * C, *t.shape[4:])

def rope_tables(rows, cols):
    quarter = RET_HEAD_DIM // 4
    freqs = ROPE_BASE ** (-jnp.arange(quarter, dtype=jnp.float32) / quarter)
    ang = jnp.concatenate([rows[:, None] * freqs, cols[:, None] * freqs], axis=-1)
    return jnp.cos(ang), jnp.sin(ang)

def rope_2d(t, cos, sin):
    half = t.shape[-1] // 2
    t1, t2 = t[..., :half], t[..., half:]
    cos = cos.astype(t.dtype)[None, None]
    sin = sin.astype(t.dtype)[None, None]
    return jnp.concatenate([t1 * cos - t2 * sin, t2 * cos + t1 * sin], axis=-1)

def conv3(t, w, b):
    tp = jnp.pad(t, ((0, 0), (1, 1), (0, 0)))
    return tp[:, :-2] * w[0] + tp[:, 1:-1] * w[1] + tp[:, 2:] * w[2] + b

def retention_scan(q, k, v, log_gamma, s0):
    idx = jnp.arange(CHUNK, dtype=jnp.float32)
    lg = log_gamma[:, None]
    k_decay = jnp.exp((CHUNK - 1 - idx) * lg)[None, :, :, None]
    q_decay = jnp.exp((idx + 1) * lg)[None, :, :, None]
    chunk_decay = jnp.exp(CHUNK * log_gamma)[None, :, None, None]
    rel = idx[:, None] - idx[None, :]
    intra = jnp.where(rel >= 0, jnp.exp(jnp.maximum(rel, 0.0) * lg[:, :, None]), 0.0)[None]
    xs = (to_chunks(k), to_chunks(v)) + (() if q is None else (to_chunks(q),))

    def step(S, blk):
        kb, vb = blk[0], blk[1]
        S_next = S * chunk_decay + jnp.einsum('bhcd,bhce->bhde', kb * k_decay, vb)
        if q is None:
            return S_next, None
        qb = blk[2]
        scores = jnp.einsum('bhid,bhjd->bhij', qb, kb) * intra
        out = (jnp.einsum('bhij,bhje->bhie', scores, vb)
               + jnp.einsum('bhid,bhde->bhie', qb * q_decay, S))
        return S_next, out

    s_fin, outs = lax.scan(step, s0, xs)
    return (None if q is None else from_chunks(outs)), s_fin

def mlstm_scan(q, k, v, i_pre, f_pre, state0):
    idx = jnp.arange(CHUNK)
    causal = (idx[:, None] >= idx[None, :])
    log_f = jax.nn.log_sigmoid(f_pre)
    xs = (to_chunks(k), to_chunks(v), to_chunks(i_pre), to_chunks(log_f)) + (
        () if q is None else (to_chunks(q),))

    def step(carry, blk):
        Cm, n, m = carry
        kb, vb, ib, lfb = blk[0], blk[1], blk[2], blk[3]
        b = jnp.cumsum(lfb, axis=-1)
        b_tot = b[..., -1]
        log_ws = b_tot[..., None] - b + ib
        m_next = jnp.maximum(b_tot + m, jnp.max(log_ws, axis=-1))
        decay_prev = jnp.exp(b_tot + m - m_next)
        ws = jnp.exp(log_ws - m_next[..., None])
        C_next = decay_prev[..., None, None] * Cm + jnp.einsum('bhcd,bhce->bhde', kb * ws[..., None], vb)
        n_next = decay_prev[..., None] * n + jnp.einsum('bhc,bhcd->bhd', ws, kb)
        if q is None:
            return (C_next, n_next, m_next), None
        qb = blk[4]
        log_w = jnp.where(causal, b[..., :, None] - b[..., None, :] + ib[..., None, :], -jnp.inf)
        log_inter = b + m[..., None]
        m_i = jnp.maximum(log_inter, jnp.max(log_w, axis=-1))
        w = jnp.exp(log_w - m_i[..., None])
        inter = jnp.exp(log_inter - m_i)
        scores = jnp.einsum('bhid,bhjd->bhij', qb, kb) * w
        num = (jnp.einsum('bhij,bhje->bhie', scores, vb)
               + inter[..., None] * jnp.einsum('bhid,bhde->bhie', qb, Cm))
        den = jnp.sum(scores, axis=-1) + inter * jnp.einsum('bhid,bhd->bhi', qb, n)
        h = num / jnp.maximum(jnp.abs(den), jnp.exp(-m_i))[..., None]
        return (C_next, n_next, m_next), h

    s_fin, outs = lax.scan(step, state0, xs)
    return (None if q is None else from_chunks(outs)), s_fin

def zero_states(B):
    r = jnp.zeros((B, RET_HEADS, RET_HEAD_DIM, RET_HEAD_DIM), jnp.float32)
    m = (jnp.zeros((B, MLSTM_HEADS, MLSTM_HEAD_DIM, MLSTM_HEAD_DIM), jnp.float32),
         jnp.zeros((B, MLSTM_HEADS, MLSTM_HEAD_DIM), jnp.float32),
         jnp.zeros((B, MLSTM_HEADS), jnp.float32))
    return (r, r, m, m)

def mixer_sublayer(h, rope, init, w_in, log_decay, ret_norm_g, conv_w, conv_b,
                   gate_b, mlstm_norm_g, w_out, with_output):
    B, N, _ = h.shape
    R, M = RET_W, MLSTM_W
    p = h @ w_in
    rq, rk, rv, rg = p[..., :R], p[..., R:2 * R], p[..., 2 * R:3 * R], p[..., 3 * R:4 * R]
    o0 = 4 * R
    mqk = jax.nn.silu(conv3(p[..., o0:o0 + 2 * M], conv_w, conv_b))
    mv = p[..., o0 + 2 * M:o0 + 3 * M]
    mo = p[..., o0 + 3 * M:o0 + 4 * M]
    gates = (p[..., o0 + 4 * M:].astype(jnp.float32) + gate_b.astype(jnp.float32).reshape(-1))
    gates = gates.reshape(B, N, 4, MLSTM_HEADS).transpose(2, 0, 3, 1)
    i_f, f_f, i_b, f_b = gates[0], gates[1], gates[2], gates[3]

    rq = split_heads(rq, RET_HEADS) * (RET_HEAD_DIM ** -0.5)
    rk = split_heads(rk, RET_HEADS)
    if rope is not None:
        rq = rope_2d(rq, *rope)
        rk = rope_2d(rk, *rope)
    rv = split_heads(rv, RET_HEADS)
    mq = split_heads(mqk[..., :M], MLSTM_HEADS)
    mk = split_heads(mqk[..., M:], MLSTM_HEADS) * (MLSTM_HEAD_DIM ** -0.5)
    mv = split_heads(mv, MLSTM_HEADS)
    log_gamma = -jnp.exp(log_decay.astype(jnp.float32))

    qr = rq if with_output else None
    qm = mq if with_output else None
    rs_f, rs_b, ms_f, ms_b = init
    ret_f, rs_f = retention_scan(qr, rk, rv, log_gamma[0], rs_f)
    ret_b, rs_b = retention_scan(flip_seq(qr), flip_seq(rk), flip_seq(rv), log_gamma[1], rs_b)
    ml_f, ms_f = mlstm_scan(qm, mk, mv, i_f, f_f, ms_f)
    ml_b, ms_b = mlstm_scan(flip_seq(qm), flip_seq(mk), flip_seq(mv), flip_seq(i_b), flip_seq(f_b), ms_b)
    states = (rs_f, rs_b, ms_f, ms_b)
    if not with_output:
        return None, states
    ret = head_norm(ret_f + flip_seq(ret_b), ret_norm_g) * jax.nn.silu(rg.astype(jnp.float32))
    mls = head_norm(ml_f + flip_seq(ml_b), mlstm_norm_g) * jax.nn.sigmoid(mo.astype(jnp.float32))
    y = jnp.concatenate([ret, mls], axis=-1).astype(h.dtype) @ w_out
    return y, states

def swiglu(t, wg, wu, wd):
    return (jax.nn.silu(t @ wg) * (t @ wu)) @ wd

def routed_experts(t, eidx, wts, w_gate, w_up, w_down):
    T, D = t.shape
    A = T * TOP_K
    e_flat = eidx.reshape(-1)
    tok_flat = jnp.repeat(jnp.arange(T, dtype=jnp.int32), TOP_K)
    w_flat = wts.reshape(-1)
    order = jnp.argsort(e_flat)
    e_s, tok_s, w_s = e_flat[order], tok_flat[order], w_flat[order]
    sizes = jnp.zeros((N_EXPERTS,), jnp.int32).at[e_flat].add(1)
    starts = jnp.cumsum(sizes) - sizes
    padded = (sizes + EXPERT_BLOCK - 1) // EXPERT_BLOCK * EXPERT_BLOCK
    pends = jnp.cumsum(padded)
    pstarts = pends - padded
    dest = pstarts[e_s] + (jnp.arange(A, dtype=jnp.int32) - starts[e_s])
    P = -(-(A + N_EXPERTS * (EXPERT_BLOCK - 1)) // EXPERT_BLOCK) * EXPERT_BLOCK
    NB = P // EXPERT_BLOCK
    buf_tok = jnp.zeros((P,), jnp.int32).at[dest].set(tok_s)
    buf_w = jnp.zeros((P,), t.dtype).at[dest].set(w_s)
    block_e = jnp.clip(jnp.searchsorted(pends, jnp.arange(NB, dtype=jnp.int32) * EXPERT_BLOCK,
                                        side='right'), 0, N_EXPERTS - 1)

    def body(y, blk):
        tok, wb, e = blk
        xb = t[tok]
        hb = jax.nn.silu(xb @ w_gate[e]) * (xb @ w_up[e])
        return y.at[tok].add((hb @ w_down[e]) * wb[:, None]), None

    y, _ = lax.scan(body, jnp.zeros_like(t),
                    (buf_tok.reshape(NB, EXPERT_BLOCK), buf_w.reshape(NB, EXPERT_BLOCK), block_e))
    return y

def moe_ffn(h, w_router, router_bias, w_gate, w_up, w_down, ws_gate, ws_up, ws_down):
    B, N, D = h.shape
    T = B * N
    t = h.reshape(T, D)
    scores = jax.nn.sigmoid((t @ w_router).astype(jnp.float32))
    sel = scores + router_bias.astype(jnp.float32)
    grp = lax.top_k(sel.reshape(T, N_GROUPS, N_EXPERTS // N_GROUPS), 2)[0].sum(-1)
    _, gidx = lax.top_k(grp, TOPK_GROUPS)
    gmask = jax.nn.one_hot(gidx, N_GROUPS, dtype=jnp.float32).sum(1) > 0
    emask = jnp.repeat(gmask, N_EXPERTS // N_GROUPS, axis=1)
    _, eidx = lax.top_k(jnp.where(emask, sel, -jnp.inf), TOP_K)
    wts = jnp.take_along_axis(scores, eidx, axis=1)
    wts = wts / jnp.sum(wts, axis=-1, keepdims=True) * ROUTED_SCALE
    routed = routed_experts(t, eidx, wts.astype(t.dtype), w_gate, w_up, w_down)
    shared = swiglu(t, ws_gate, ws_up, ws_down)
    return (routed + shared).reshape(B, N, D)

def setup_inputs(seed: int = 0) -> dict:
    key = jax.random.key(seed)
    ks = jax.random.split(key, 24)
    f32 = jnp.float32

    def nrm(k, shape, scale):
        return jax.random.normal(k, shape, f32) * scale

    D = D_MODEL
    decay_base = jnp.asarray(np.log(-np.log(1.0 - 2.0 ** (-5.0 - np.arange(RET_HEADS)))), dtype=f32)
    fb = jnp.linspace(3.0, 6.0, MLSTM_HEADS, dtype=f32)
    zb = jnp.zeros((MLSTM_HEADS,), f32)
    gate_base = jnp.stack([zb, fb, zb, fb])
    return {
        'x': nrm(ks[0], (BATCH, SEQ, D), 1.0),
        'c': nrm(ks[1], (BATCH, D), 1.0),
        'ctx': nrm(ks[2], (BATCH, CTX_LEN, D), 1.0),
        'c_ctx': nrm(ks[3], (D,), 1.0),
        'w_mod': nrm(ks[4], (DEPTH, D, N_MOD * D), D ** -0.5),
        'b_mod': nrm(ks[5], (DEPTH, N_MOD * D), 0.02),
        'norm_g': 1.0 + nrm(ks[6], (DEPTH, 4, D), 0.05),
        'w_in': nrm(ks[7], (DEPTH, D, IN_COLS), D ** -0.5),
        'ret_log_decay': decay_base[None, None, :] + nrm(ks[8], (DEPTH, 2, RET_HEADS), 0.1),
        'ret_norm_g': 1.0 + nrm(ks[9], (DEPTH, RET_W), 0.05),
        'mlstm_conv_w': nrm(ks[10], (DEPTH, CONV_W, 2 * MLSTM_W), CONV_W ** -0.5),
        'mlstm_conv_b': nrm(ks[11], (DEPTH, 2 * MLSTM_W), 0.02),
        'mlstm_gate_b': gate_base[None] + nrm(ks[12], (DEPTH, 4, MLSTM_HEADS), 0.1),
        'mlstm_norm_g': 1.0 + nrm(ks[13], (DEPTH, MLSTM_W), 0.05),
        'w_out': nrm(ks[14], (DEPTH, MIX_W, D), MIX_W ** -0.5),
        'w_router': nrm(ks[15], (DEPTH, D, N_EXPERTS), D ** -0.5),
        'router_bias': nrm(ks[16], (DEPTH, N_EXPERTS), 0.01),
        'w_gate': nrm(ks[17], (DEPTH, N_EXPERTS, D, EXPERT_FF), D ** -0.5),
        'w_up': nrm(ks[18], (DEPTH, N_EXPERTS, D, EXPERT_FF), D ** -0.5),
        'w_down': nrm(ks[19], (DEPTH, N_EXPERTS, EXPERT_FF, D), EXPERT_FF ** -0.5),
        'ws_gate': nrm(ks[20], (DEPTH, D, SHARED_FF), D ** -0.5),
        'ws_up': nrm(ks[21], (DEPTH, D, SHARED_FF), D ** -0.5),
        'ws_down': nrm(ks[22], (DEPTH, SHARED_FF, D), SHARED_FF ** -0.5),
    }

def reference(x, c, ctx, c_ctx, w_mod, b_mod, norm_g, w_in, ret_log_decay, ret_norm_g,
              mlstm_conv_w, mlstm_conv_b, mlstm_gate_b, mlstm_norm_g, w_out, w_router,
              router_bias, w_gate, w_up, w_down, ws_gate, ws_up, ws_down):
    B, N, D = x.shape
    ROWS = N // GRID_W
    rows = jnp.repeat(jnp.arange(ROWS, dtype=jnp.float32), GRID_W)
    cols = jnp.tile(jnp.arange(GRID_W, dtype=jnp.float32), ROWS)
    rope = rope_tables(rows, cols)
    for l in range(DEPTH):
        last = l == DEPTH - 1
        mod = (jax.nn.silu(c) @ w_mod[l] + b_mod[l]).reshape(B, N_MOD, D)
        sh1, sc1, g1, sh2, sc2, g2 = [mod[:, i][:, None, :] for i in range(N_MOD)]
        mod_c = (jax.nn.silu(c_ctx) @ w_mod[l] + b_mod[l]).reshape(N_MOD, D)
        csh1, csc1, cg1, csh2, csc2, cg2 = [mod_c[i] for i in range(N_MOD)]
        mix_params = (w_in[l], ret_log_decay[l], ret_norm_g[l], mlstm_conv_w[l], mlstm_conv_b[l],
                      mlstm_gate_b[l], mlstm_norm_g[l], w_out[l])
        h_ctx = modulate(rmsnorm(ctx, norm_g[l, 0]), csh1, csc1)
        y_ctx, ctx_states = mixer_sublayer(h_ctx, None, zero_states(ctx.shape[0]), *mix_params,
                                           with_output=not last)
        h_lat = modulate(rmsnorm(x, norm_g[l, 0]), sh1, sc1)
        y_lat, _ = mixer_sublayer(h_lat, rope, ctx_states, *mix_params, with_output=True)
        x = x + g1 * rmsnorm(y_lat, norm_g[l, 1])
        moe_params = (w_router[l], router_bias[l], w_gate[l], w_up[l], w_down[l],
                      ws_gate[l], ws_up[l], ws_down[l])
        if not last:
            ctx = ctx + cg1 * rmsnorm(y_ctx, norm_g[l, 1])
            hc = modulate(rmsnorm(ctx, norm_g[l, 2]), csh2, csc2)
            ctx = ctx + cg2 * rmsnorm(moe_ffn(hc, *moe_params), norm_g[l, 3])
        h = modulate(rmsnorm(x, norm_g[l, 2]), sh2, sc2)
        x = x + g2 * rmsnorm(moe_ffn(h, *moe_params), norm_g[l, 3])
    return x


_drawn_inputs = setup_inputs


def setup_inputs(seed=0):
    import zlib

    import numpy as np

    out = dict(_drawn_inputs(seed))
    spreads = {}
    factors = {'mlstm_conv_b': 6.794}
    for name, (base, spread) in spreads.items():
        noise = np.random.default_rng([zlib.crc32(name.encode()), seed]).standard_normal(out[name].shape)
        drawn = base * np.exp(spread * noise) if base else spread * noise
        out[name] = jnp.asarray(drawn.astype(out[name].dtype))
    for name, factor in factors.items():
        out[name] = (out[name] * factor).astype(out[name].dtype)
    return out
```

```python
from contextlib import ExitStack

import numpy as np

import concourse.bass as bass
from concourse import mybir

F32 = mybir.dt.float32
I32 = mybir.dt.int32
U32 = mybir.dt.uint32
ALU = mybir.AluOpType
ACT = mybir.ActivationFunctionType
AX = mybir.AxisListType

P = 128
D = 1024
KD = D // P
SEQ, CTX = 512, 256
TL, TC = SEQ // P, CTX // P
H = 4
HD = 128
W = H * HD
CHUNKS = TL + TC
GRID_W = 64
NE, TOPK, NG = 64, 8, 8
FF = 256
ROUTED_SCALE = 2.5
EPS = 1e-6
SCALE = HD ** -0.5
BIG = 1e30
U = 3
MAX_BLOCKS = NE + SEQ * TOPK // P - 1
ITERS = -(-MAX_BLOCKS // U)
LIST = U * ITERS + 2
CODES = NE + 1
LEVELS = SEQ // P
TRASH = SEQ

CONST = {}
_at = 0
for _name, _n in [("ident", P), ("iota", P), ("ones", P), ("le", P), ("lt", P), ("relp", P), ("reln", P),
                  ("negf", P), ("negb", P), ("ge", P), ("p", 1), ("rp", 1), ("p1", 1), ("rp1", 1),
                  ("trash", 1), ("tok1", TL), ("eps", 1), ("sel", H * P), ("cos", TL * 64), ("sin", TL * 64)]:
    CONST[_name] = (_at, _at + _n)
    _at += _n
NCONST = _at


def constants():
    c = np.zeros((P, NCONST), np.float32)
    p = np.arange(P, dtype=np.float32)[:, None]
    m = np.arange(P, dtype=np.float32)[None, :]

    def put(name, v):
        a, b = CONST[name]
        c[:, a:b] = v
    put("ident", np.eye(P))
    put("iota", np.broadcast_to(m, (P, P)))
    put("ones", 1.0)
    put("le", p <= m)
    put("lt", p < m)
    put("ge", p >= m)
    put("relp", np.maximum(m - p, 0))
    put("reln", np.maximum(p - m, 0))
    put("negf", np.where(m >= p, 0.0, BIG))
    put("negb", np.where(m <= p, 0.0, BIG))
    put("p", p)
    put("rp", P - 1 - p)
    put("p1", p + 1)
    put("rp1", P - p)
    put("trash", TRASH + 1 + p)
    put("tok1", p + 1 + P * np.arange(TL)[None, :])
    put("eps", EPS)
    sel = np.zeros((P, H, P), np.float32)
    for h in range(H):
        sel[h, h] = 1.0
    put("sel", sel.reshape(P, -1))
    quarter = HD // 4
    freqs = np.float32(10000.0) ** (-np.arange(quarter, dtype=np.float32) / np.float32(quarter))
    tok = np.arange(SEQ)
    ang = np.concatenate([(tok // GRID_W).astype(np.float32)[:, None] * freqs,
                          (tok % GRID_W).astype(np.float32)[:, None] * freqs], -1).astype(np.float32)
    lay = lambda a: a.reshape(TL, P, 64).transpose(1, 0, 2).reshape(P, -1)
    put("cos", lay(np.cos(ang)))
    put("sin", lay(np.sin(ang)))
    return c


def project_jobs():
    jobs = [("vec", None, 0)]
    jobs += [("mod1", s, s) for s in range(4)]
    jobs += [("modT", None, 0)]
    for k in range(KD):
        jobs += [("xT", None, k), ("xcT", None, k)]
    jobs += [("mk", 4, h) for h in range(H)] + [("mkc", 4, h) for h in range(H)]
    jobs += [("gate", None, 0)]
    jobs += [("mv", 5, t) for t in range(TL + TC)]
    jobs += [("mkT", None, t) for t in range(TL + TC)]
    jobs += [("rk", 6, t) for t in range(TL + TC)]
    jobs += [("rv", 7, t) for t in range(TL + TC)]
    jobs += [("rkT", None, t) for t in range(TL)]
    jobs += [("mq", 8, h) for h in range(H)]
    jobs += [("rq", 9, t) for t in range(2)]
    jobs += [("rqT", None, t) for t in range(0)]
    jobs += [("rqT", None, 0), ("rq", 9, 2), ("rqT", None, 1), ("rq", 9, 3)]
    jobs += [("rg", 10, t) for t in range(TL)]
    jobs += [("rqT", None, 2), ("rqT", None, 3)]
    jobs += [("mo", 11, t) for t in range(TL)]
    jobs += [("mod2", 12 + s, s) for s in range(8)]
    return jobs


IN_SLABS = {4: 5 * W, 5: 6 * W, 6: W, 7: 2 * W, 8: 4 * W, 9: 0, 10: 3 * W, 11: 7 * W}
SLABS = 20
NSLOT = 3
NBANK = 6


def build(nc, t, out, upto=5):
    ctx = ExitStack()
    with ctx:
        def sb(name, shape, dt=F32):
            return ctx.enter_context(nc.sbuf_tensor(name, shape, dt))

        def sem(name):
            return ctx.enter_context(nc.semaphore(name))

        h_dram = nc.dram_tensor("h_rows", (SEQ, D), F32, kind="Internal").ap()
        y_dram = nc.dram_tensor("y_rows", (SEQ + P, D), F32, kind="Internal").ap()
        m_dram = nc.dram_tensor("mod_rows", (4, D), F32, kind="Internal").ap()

        CT = sb("CT", [P, NCONST])
        X = sb("X", [P, TL, D])
        RING = sb("RING", [P, U * 6144])
        PR = sb("PR", [P, 24600])
        ST = sb("ST", [P, 2056])
        DM = sb("DM", [P, H, P])
        VECT = sb("VECT", [P, 72])
        CC = sb("CC", [P, 2, KD])
        MM = sb("MM", [P, 2, 16])
        MODA = sb("MODA", [P, 2, KD])
        SS = sb("SS", [P, 6])
        RST = sb("RST", [P, 6])
        WG = sb("WG", [P, KD, 16])
        GT = sb("GT", [P, CHUNKS, 16])
        COL = sb("COL", [P, 12, 16])
        LG = sb("LG", [P, 8])
        RARG = sb("RARG", [P, 3, 8])
        RDEC = sb("RDEC", [P, 3, 8])
        DPB = sb("DPB", [P, H, 12])
        GB = sb("GB", [4, 4])
        MST = sb("MST", [4, 2, 8])
        DEN = sb("DEN", [P, 12])
        BLI = sb("BLI", [1, 2 * LIST + 1], I32)
        IDX = sb("IDX", [P, U, 2], U32)
        WCOL = sb("WCOL", [P, U, 1])
        RHS = sb("RHS", [P, U, TL, 3])

        PS = ctx.enter_context(nc.psum_tensor("PS", [P, 8, 512], F32))

        def const(name, rows=P):
            a, b = CONST[name]
            return CT[0:rows, a:b]

        def ring(a, n, rows=P):
            return RING[0:rows, a:a + n]

        def pr(a, n, rows=P):
            return PR[0:rows, a:a + n]

        def heads(ap, m=HD):
            return ap.rearrange("p (t h d) -> p t h d", h=H, d=m)

        ident = const("ident")
        cos = const("cos").rearrange("p (t d) -> p t d", t=TL)
        sin = const("sin").rearrange("p (t d) -> p t d", t=TL)
        sel = const("sel").rearrange("p (h m) -> p h m", h=H)

        slab = [ring(s * 4096, 4096).rearrange("p (k n) -> p k n", k=KD) for s in range(NSLOT)]
        HT = ring(12288, 4096).rearrange("p (k n) -> p k n", k=KD)
        HTC = ring(16384, 2048).rearrange("p (k n) -> p k n", k=KD)

        RK = heads(pr(0, 2048))
        RV = heads(pr(2048, 2048))
        MQT = pr(4096, 2048).rearrange("p (h n) -> p h n", h=H)
        MKT = pr(6144, 2048).rearrange("p (h n) -> p h n", h=H)
        MK = heads(pr(8192, 2048))
        RQT = pr(10240, 2048).rearrange("p (h n) -> p h n", h=H)
        RKT = pr(12288, 2048).rearrange("p (h n) -> p h n", h=H)
        MV = heads(pr(14336, 2064), 129)
        RKC = heads(pr(16400, 1024))
        RVC = heads(pr(17424, 1024))
        MVC = heads(pr(18448, 1032), 129)
        MKC = heads(pr(19480, 1024))
        RG = pr(20504, 2048).rearrange("p (t n) -> p t n", t=TL)
        MO = pr(22552, 2048).rearrange("p (t n) -> p t n", t=TL)
        MKTC = pr(10240, 1024).rearrange("p (h n) -> p h n", h=H)
        XN = pr(12288, 6144).rearrange("p (t n) -> p t n", t=6)
        XC = pr(4096, 2048).rearrange("p (t n) -> p t n", t=TC)
        VEC = ring(0, P, 72)
        MODROW = ST[0:2, 0:2048]
        ACC = ST[:, 0:1024].rearrange("p (b n) -> p b n", b=2)
        RQS = ST[:, 1024:2048].rearrange("p (b n) -> p b n", b=2)
        TMP1 = pr(22552, 1024).rearrange("p (b n) -> p b n", b=2)

        jobs = project_jobs()
        at = {(what, i): n for n, (what, _, i) in enumerate(jobs)}
        last_of_slab = {s: n for n, (_, s, _) in enumerate(jobs) if s is not None}

        w_mod_v = t["w_mod"][0].rearrange("(k p) n -> p k n", p=P)
        w_in_v = t["w_in"][0].rearrange("(k p) n -> p k n", p=P)

        ld_const, ld_vec, ld_x, ld_xc, ld_wg = (sem(n) for n in ("ld_const", "ld_vec", "ld_x", "ld_xc", "ld_wg"))
        slab_ld = [sem(f"slab_ld{s}") for s in range(NSLOT)]
        ps_full = sem("ps_full")
        ps_free = [sem(f"ps_free{b}") for b in range(NBANK)]
        cc_ok, ss_ok, std_ok, xn_ok, moda_ok, silu_ok, rope_own = (sem(n) for n in (
            "cc_ok", "ss_ok", "std_ok", "xn_ok", "moda_ok", "silu_ok", "rope_own"))
        ld_small, rarg_ok, rdec_ok, em_ok, em_used = (sem(n) for n in (
            "ld_small", "rarg_ok", "rdec_ok", "em_ok", "em_used"))
        ms_st = [sem(f"ms_st{i}") for i in range(2)]
        dve_own, act_own, pool_own = (sem(n) for n in ("dve_own", "act_own", "pool_own"))

        def own(eng, s, count, ins):
            count[0] += 1
            ins.then_inc(s, 1)
            eng.wait_ge(s, count[0])

        dve_n, act_n, pool_n = [0], [0], [0]

        def evacuated(eng, n):
            eng.wait_ge(ps_free[n % NBANK], n // NBANK + 1)

        def hT_tile(i, k):
            return HT[:, k, i * P:(i + 1) * P] if i < TL else HTC[:, k, (i - TL) * P:(i - TL + 1) * P]

        def decay_tmp(n):
            return TMP1[:, n % 2, 0:P]

        with nc.Block() as block:
            @block.sync
            def _(sp):
                for name, rows, at_row in (("c", 8, 0), ("c_ctx", 8, 8), ("norm0", 8, 16), ("bmod0", 16, 24),
                                           ("conv_w", 24, 40), ("conv_b", 8, 64)):
                    src = {"c": t["c"][0, :], "c_ctx": t["c_ctx"], "norm0": t["norm_g"][0, 0, :],
                           "bmod0": t["b_mod"][0, 0:2048], "conv_w": t["mlstm_conv_w"][0].rearrange("a n -> (a n)"),
                           "conv_b": t["mlstm_conv_b"][0]}[name]
                    sp.dma_start(VEC[at_row:at_row + rows, :], src.rearrange("(r n) -> r n", n=P)).then_inc(ld_vec, 16)
                sp.dma_start(CT[:, :], t["consts"]).then_inc(ld_const, 16)
                for n in range(SLABS):
                    slot = n % NSLOT
                    if n == 0:
                        sp.wait_ge(ps_full, 1)
                    if n >= NSLOT:
                        sp.wait_ge(ps_full, last_of_slab[n - NSLOT] + 1)
                    if n < 4:
                        src = w_mod_v[:, :, n * 512:(n + 1) * 512]
                    elif n < 12:
                        src = w_in_v[:, :, IN_SLABS[n]:IN_SLABS[n] + 512]
                    else:
                        src = w_mod_v[:, :, (n - 8) * 512:(n - 7) * 512]
                    sp.dma_start(slab[slot], src).then_inc(slab_ld[slot], 16)

            @block.gpsimd
            def _(pool):
                pool.wait_ge(ps_full, at["xcT", KD - 1] + 1)
                nc.gpsimd.memset(MV[:, :, :, HD:HD + 1], 1.0)
                nc.gpsimd.memset(MVC[:, :, :, HD:HD + 1], 1.0)

            @block.scalar
            def _(act):
                act.dma_start(X[:, :, :], t["x"][0].rearrange("(t p) n -> p t n", p=P)).then_inc(ld_x, 16)
                act.dma_start(XC, t["ctx"][0].rearrange("(t p) n -> p t n", p=P)).then_inc(ld_xc, 16)
                act.dma_start(LG[:, :], t["ret_log_decay"][0].rearrange("a h -> (a h)").partition_broadcast(P)).then_inc(ld_small, 16)
                act.dma_start(WG[:, :, :], w_in_v[:, :, 8 * W:8 * W + 16]).then_inc(ld_wg, 16)
                act.wait_ge(ld_x, 16)
                for i in range(TL):
                    nc.scalar.activation(XN[:, i, :], X[:, i, :], ACT.Square, accum_out=SS[:, i:i + 1]).then_inc(ss_ok, 1)
                act.wait_ge(ld_xc, 16)
                for i in range(TC):
                    nc.scalar.activation(XN[:, TL + i, :], XC[:, i, :], ACT.Square, accum_out=SS[:, TL + i:TL + i + 1]).then_inc(ss_ok, 1)
                act.wait_ge(ss_ok, 6)
                act.wait_ge(ld_const, 16)
                nc.scalar.activation(RST[:, :], SS[:, :], ACT.Sqrt, bias=const("eps"), scale=1.0 / D).then_inc(std_ok, 1)
                act.wait_ge(ld_small, 16)
                own(act, act_own, act_n, nc.scalar.activation(RARG[:, 0, :], LG[:, :], ACT.Exp))
                own(act, act_own, act_n, nc.scalar.mul(LG[:, :], RARG[:, 0, :], -1.0))
                act.wait_ge(rarg_ok, 1)
                nc.scalar.activation(RDEC[:, :, :], RARG[:, :, :], ACT.Exp).then_inc(rdec_ok, 1)
                for h in range(H):
                    for d, rel in enumerate(("relp", "reln")):
                        n = 2 * h + d
                        if n >= 2:
                            act.wait_ge(em_used, n - 1)
                        nc.scalar.activation(decay_tmp(n), const(rel), ACT.Exp, scale=LG[:, d * 4 + h:d * 4 + h + 1]).then_inc(em_ok, 1)
                n_silu = 0
                for n, (what, _, i) in enumerate(jobs):
                    bank = n % NBANK
                    full = PS[:, bank, :]
                    if what == "vec":
                        evacuated(act, n)
                        nc.scalar.activation(CC[:, :, :].rearrange("p s k -> p (s k)"), VECT[:, 0:16], ACT.Silu).then_inc(cc_ok, 1)
                        continue
                    if what == "modT":
                        act.wait_ge(moda_ok, 1)
                        continue
                    if what == "rq" or what == "rk" and i < TL:
                        continue
                    if what in ("mk", "mkc", "mq"):
                        evacuated(act, n)
                        dst = {"mk": MKT[:, i, :], "mkc": MKTC[:, i, :], "mq": MQT[:, i, :]}[what]
                        nc.scalar.activation(dst, ACC[:, n_silu % 2, 0:(CTX if what == "mkc" else SEQ)], ACT.Silu).then_inc(silu_ok, 1)
                        n_silu += 1
                        continue
                    act.wait_ge(ps_full, n + 1)
                    if what == "mod1":
                        ins = nc.scalar.copy(MODROW[:, i * 512:(i + 1) * 512], PS[0:2, bank, :])
                    elif what == "xT":
                        ins = nc.scalar.activation(HT[:, i, :], full, ACT.Identity, bias=MM[:, 0, i:i + 1], scale=MODA[:, 0, i:i + 1])
                    elif what == "xcT":
                        ins = nc.scalar.activation(HTC[:, i, :], full[:, 0:CTX], ACT.Identity, bias=MM[:, 1, i:i + 1], scale=MODA[:, 1, i:i + 1])
                    elif what == "gate":
                        ins = nc.scalar.copy(GT[:, :, :].rearrange("p c n -> p (c n)"), full[:, 0:96])
                    elif what in ("mv", "rv", "rk"):
                        lat, cx = {"mv": (MV, MVC), "rv": (RV, RVC), "rk": (RK, RKC)}[what]
                        dst = lat[:, i] if i < TL else cx[:, i - TL]
                        ins = nc.scalar.copy(dst[:, :, 0:HD], full.rearrange("p (h d) -> p h d", h=H))
                    elif what == "mkT":
                        dst = MK[:, i] if i < TL else MKC[:, i - TL]
                        ins = nc.scalar.copy(dst, full.rearrange("p (h d) -> p h d", h=H))
                    elif what in ("rkT", "rqT"):
                        dst = (RKT if what == "rkT" else RQT)[:, :, i * P:(i + 1) * P]
                        ins = nc.scalar.copy(dst, full.rearrange("p (h d) -> p h d", h=H))
                    elif what == "rg":
                        ins = nc.scalar.activation(RG[:, i, :], full, ACT.Silu)
                    elif what == "mo":
                        ins = nc.scalar.activation(MO[:, i, :], full, ACT.Sigmoid)
                    elif what == "mod2":
                        if i >= 2:
                            act.wait_ge(ms_st[i % 2], 16 * (i // 2))
                        ins = nc.scalar.copy(ACC[0:1, i % 2, :], full[0:1, :])
                    ins.then_inc(ps_free[bank], 1)
                    if what == "mod2":
                        evacuated(act, n)
                        act.dma_start(m_dram[i // 2:i // 2 + 1, (i % 2) * 512:(i % 2 + 1) * 512], ACC[0:1, i % 2, :]).then_inc(ms_st[i % 2], 16)
                for s in ms_st:
                    act.wait_ge(s, 16 * 4)

            @block.vector
            def _(dve):
                def o(ins):
                    own(dve, dve_own, dve_n, ins)
                dve.wait_ge(ld_const, 16)
                dve.wait_ge(act_own, 2)
                for a, (f, b) in enumerate((("rp", "p"), ("p1", "rp1"))):
                    nc.vector.tensor_scalar(RARG[:, a, 0:4], LG[:, 0:4], const(f), None, ALU.mult)
                    nc.vector.tensor_scalar(RARG[:, a, 4:8], LG[:, 4:8], const(b), None, ALU.mult)
                nc.vector.tensor_scalar(RARG[:, 2, :], LG[:, :], float(P), None, ALU.mult).then_inc(rarg_ok, 1)
                dve.wait_ge(rdec_ok, 1)
                o(nc.vector.tensor_scalar(RDEC[:, 1, :], RDEC[:, 1, :], SCALE, None, ALU.mult))
                for h in range(H):
                    for d, mask in enumerate(("le", "ge")):
                        n = 2 * h + d
                        dve.wait_ge(em_ok, n + 1)
                        if d == 0:
                            ins = nc.vector.scalar_tensor_tensor(out=DM[:, h, :], in0=decay_tmp(n), scalar=SCALE, in1=const(mask), op0=ALU.mult, op1=ALU.mult)
                        else:
                            o(nc.vector.scalar_tensor_tensor(out=decay_tmp(n), in0=decay_tmp(n), scalar=SCALE, in1=const(mask), op0=ALU.mult, op1=ALU.mult))
                            ins = nc.vector.tensor_tensor(DM[:, h, :], DM[:, h, :], decay_tmp(n), ALU.add)
                        ins.then_inc(em_used, 1)
                        dve.wait_ge(em_used, n + 1)
                dve.wait_ge(std_ok, 1)
                o(nc.vector.reciprocal(RST[:, :], RST[:, :]))
                for i in range(6):
                    src = X[:, i, :] if i < TL else XC[:, i - TL, :]
                    nc.vector.tensor_scalar(XN[:, i, :], src, RST[:, i:i + 1], None, ALU.mult).then_inc(xn_ok, 1)
                n_conv = n_rope = 0
                for n, (what, _, i) in enumerate(jobs):
                    bank = n % NBANK
                    full = PS[:, bank, :]
                    if what == "vec":
                        dve.wait_ge(ps_full, n + 1)
                        nc.vector.tensor_copy(VECT[:, :], full[:, 0:72]).then_inc(ps_free[bank], 1)
                        evacuated(dve, n)
                    elif what == "modT":
                        dve.wait_ge(ps_full, n + 1)
                        mt = full[:, 0:32].rearrange("p (c s) -> p s c", s=2)
                        bmod = VECT[:, 24:40].unsqueeze(1).to_broadcast([P, 2, 16])
                        ng0 = VECT[:, 16:24].unsqueeze(1).to_broadcast([P, 2, KD])
                        nc.vector.tensor_tensor(MM[:, :, :], mt, bmod, ALU.add).then_inc(ps_free[bank], 1)
                        evacuated(dve, n)
                        nc.vector.scalar_tensor_tensor(out=MODA[:, :, :], in0=MM[:, :, 8:16], scalar=1.0, in1=ng0,
                                                       op0=ALU.add, op1=ALU.mult).then_inc(moda_ok, 1)
                    elif what in ("mk", "mkc", "mq"):
                        dve.wait_ge(ps_full, n + 1)
                        N = CTX if what == "mkc" else SEQ
                        f = (0 if what == "mq" else H) + i
                        w = [VECT[:, 40 + 8 * j + f:41 + 8 * j + f] for j in range(3)]
                        acc = ACC[:, n_conv % 2, 0:N]
                        if n_conv >= 2:
                            dve.wait_ge(silu_ok, n_conv - 1)
                        o(nc.vector.tensor_scalar(acc, full[:, 0:N], w[1], VECT[:, 64 + f:65 + f], ALU.mult, ALU.add))
                        o(nc.vector.scalar_tensor_tensor(out=acc[:, 1:N], in0=full[:, 0:N - 1], scalar=w[0], in1=acc[:, 1:N], op0=ALU.mult, op1=ALU.add))
                        nc.vector.scalar_tensor_tensor(out=acc[:, 0:N - 1], in0=full[:, 1:N], scalar=w[2], in1=acc[:, 0:N - 1],
                                                       op0=ALU.mult, op1=ALU.add).then_inc(ps_free[bank], 1)
                        n_conv += 1
                    elif what == "rq" or what == "rk" and i < TL:
                        dve.wait_ge(ps_full, n + 1)
                        ph = full.rearrange("p (h s d) -> p h s d", h=H, s=2)
                        cs, sn = (a[:, i, :].unsqueeze(1).to_broadcast([P, H, 64]) for a in (cos, sin))
                        if what == "rk":
                            dst = RK[:, i]
                        else:
                            if i >= 2:
                                dve.wait_ge(ps_full, at["rqT", i - 2] + 1)
                            dst = RQS[:, i % 2, :].rearrange("p (h d) -> p h d", h=H)
                        a, b = (TMP1[:, j, :].rearrange("p (h s d) -> p h s d", h=H, s=2) for j in range(2))
                        for s in range(2):
                            nc.vector.tensor_tensor(a[:, :, s, :], ph[:, :, s, :], cs, ALU.mult)
                            nc.vector.tensor_tensor(b[:, :, s, :], ph[:, :, 1 - s, :], sn, ALU.mult).then_inc(rope_own, 1)
                        dve.wait_ge(rope_own, 2 * n_rope + 2)
                        nc.vector.tensor_tensor(dst[:, :, 0:64], a[:, :, 0, :], b[:, :, 0, :], ALU.subtract)
                        nc.vector.tensor_tensor(dst[:, :, 64:128], a[:, :, 1, :], b[:, :, 1, :], ALU.add).then_inc(ps_free[bank], 1)
                        n_rope += 1
                        evacuated(dve, n)

            @block.tensor
            def _(pe):
                pe.wait_ge(ld_const, 16)
                pe.wait_ge(ld_vec, 16 * 6)
                for n, (what, s, i) in enumerate(jobs):
                    bank = n % NBANK
                    full = PS[:, bank, :]
                    if n >= NBANK:
                        pe.wait_ge(ps_free[bank], n // NBANK)
                    if s is not None:
                        pe.wait_ge(slab_ld[s % NSLOT], 16 * (s // NSLOT + 1))
                        w = slab[s % NSLOT]
                    if what == "vec":
                        last = nc.tensor.transpose(full[:, 0:72], VEC, const("ident", 72)[:, 0:72])
                    elif what in ("mod1", "mod2"):
                        pe.wait_ge(cc_ok, 1)
                        m = 2 if what == "mod1" else 1
                        for k in range(KD):
                            last = nc.tensor.matmul(full[0:m, :], CC[:, 0:m, k], w[:, k, :], start=k == 0, stop=k == KD - 1)
                    elif what == "modT":
                        for s1 in range(4):
                            evacuated(pe, at["mod1", s1])
                        for c in range(16):
                            last = nc.tensor.transpose(full[:, 2 * c:2 * c + 2], MODROW[:, c * P:(c + 1) * P], const("ident", 2)[:, 0:2])
                    elif what in ("xT", "xcT"):
                        pe.wait_ge(xn_ok, 6)
                        for c in range(TL if what == "xT" else TC):
                            src = XN[:, c if what == "xT" else TL + c, i * P:(i + 1) * P]
                            last = nc.tensor.transpose(full[:, c * P:(c + 1) * P], src, ident)
                    elif what in ("mk", "mkc", "mq"):
                        evacuated(pe, at["xcT", KD - 1])
                        h = HTC if what == "mkc" else HT
                        N = CTX if what == "mkc" else SEQ
                        for k in range(KD):
                            last = nc.tensor.matmul(full[:, 0:N], w[:, k, i * HD:(i + 1) * HD], h[:, k, :], start=k == 0, stop=k == KD - 1)
                    elif what == "gate":
                        pe.wait_ge(ld_wg, 16)
                        for c in range(TL + TC):
                            for k in range(KD):
                                last = nc.tensor.matmul(full[:, c * 16:(c + 1) * 16], hT_tile(c, k), WG[:, k, :], start=k == 0, stop=k == KD - 1)
                    elif what == "mkT":
                        pe.wait_ge(silu_ok, 2 * H)
                        src = MKT[:, :, i * P:(i + 1) * P] if i < TL else MKTC[:, :, (i - TL) * P:(i - TL + 1) * P]
                        for h in range(H):
                            last = nc.tensor.transpose(full[:, h * HD:(h + 1) * HD], src[:, h, :], ident)
                    elif what in ("rkT", "rqT"):
                        evacuated(pe, at[what[:2], i])
                        src = RK[:, i] if what == "rkT" else RQS[:, i % 2, :].rearrange("p (h d) -> p h d", h=H)
                        for h in range(H):
                            last = nc.tensor.transpose(full[:, h * HD:(h + 1) * HD], src[:, h, :], ident)
                    else:
                        for k in range(KD):
                            last = nc.tensor.matmul(full, hT_tile(i, k), w[:, k, :], start=k == 0, stop=k == KD - 1)
                    last.then_inc(ps_full, 1)
        if upto == 1:
            return

        UNITS = 2 * CHUNKS
        STEPS = CHUNKS

        def chunk_of(n):
            s, d = divmod(n, 2)
            if s < TC:
                return False, (s if d == 0 else TC - 1 - s)
            return True, (s - TC if d == 0 else TL - 1 - (s - TC))

        def pos_of(n):
            lat, c = chunk_of(n)
            return TC + c if lat else c

        KINDS = {
            "all": list(range(UNITS)),
            "lat": [n for n in range(UNITS) if n // 2 >= TC],
            "intra": [n for n in range(UNITS) if TC <= n // 2 < TC + TL // 2],
            "state": [n for n in range(UNITS) if n // 2 < STEPS - 1],
        }

        def upto_unit(kind, n):
            return sum(u <= n for u in KINDS[kind])

        def wait(eng, s, v):
            if v > 0:
                eng.wait_ge(s, v)

        def rows4(a, n):
            return ring(a, n, 4)

        GR = rows4(0, 3072).rearrange("p (k n) -> p k n", k=4)
        BB = rows4(3072, 1536).rearrange("p (d n) -> p d n", d=2)
        AR = rows4(4608, 1536).rearrange("p (d n) -> p d n", d=2)
        AA = rows4(6144, 1536).rearrange("p (d n) -> p d n", d=2)
        TT = ring(7680, 1536)
        LF = rows4(9216, 1536).rearrange("p (d n) -> p d n", d=2)
        ZF = rows4(10752, 1536).rearrange("p (d n) -> p d n", d=2)
        W1, W2 = LF, ZF
        W3 = rows4(0, 1536).rearrange("p (d n) -> p d n", d=2)
        TTd = TT.rearrange("p (d n) -> p d n", d=2)
        DPE = sb("DPE", [4, 12])
        OR = ring(12288, 2048).rearrange("p (t h n) -> p t h n", t=TL, h=H)
        OM = ring(14336, 2048).rearrange("p (t h n) -> p t h n", t=TL, h=H)
        PT = ring(16384, 512).rearrange("p (h n) -> p h n", h=H)
        KDB = ring(16896, 512).rearrange("p (h n) -> p h n", h=H)
        ZE = ring(17408, 512).rearrange("p (h n) -> p h n", h=H)
        PT2 = ring(17920, 512).rearrange("p (h n) -> p h n", h=H)
        KWB = ring(9216, 512).rearrange("p (h n) -> p h n", h=H)
        TI = ring(9728, 516).rearrange("p (a n) -> p a n", a=2)
        ND = ring(10752, 516)
        SR = ST[:, 0:1024].rearrange("p (d h n) -> p d h n", d=2, h=H)
        SM = ST[:, 1024:2056].rearrange("p (d h n) -> p d h n", d=2, h=H)
        ND4 = ND.rearrange("p (h n) -> p h n", h=H)
        TI4 = ring(9728, 516).rearrange("p (h n) -> p h n", h=H)

        ld_gb, gT_full, gT_out, rows_ok, nl_ok, exp_ok, tt_ok, tt_zero = (sem(n) for n in (
            "ld_gb", "gT_full", "gT_out", "rows_ok", "nl_ok", "exp_ok", "tt_ok", "tt_zero"))
        col_full, col_ok, dpb_full, dpb_ok = (sem(n) for n in ("col_full", "col_ok", "dpb_full", "dpb_ok"))
        r_sc, r_out, r_in, r_st, m_qk, m_a, m_num, m_in, m_st = (sem("pe_" + n) for n in (
            "r_sc", "r_out", "r_in", "r_st", "m_qk", "m_a", "m_num", "m_in", "m_st"))
        pt_ok, or_ok, s_ok, z_ok, pt2_ok, nd_ok, c_ok, om_ok = (sem("dve_" + n) for n in (
            "pt", "or", "s", "z", "pt2", "nd", "c", "om"))
        ro_ok, kd_ok, e_ok, kw_ok, ti_ok = (sem("act_" + n) for n in ("ro", "kd", "e", "kw", "ti"))

        with nc.Block() as block:
            @block.sync
            def _(sp):
                with nc.allow_non_contiguous_dma(reason="sixteen gate biases"):
                    sp.dma_start(GB[:, :], t["mlstm_gate_b"][0].rearrange("g h -> h g")).then_inc(ld_gb, 16)

            @block.gpsimd
            def _(pool):
                nc.gpsimd.memset(TT, 0.0).then_inc(tt_zero, 1)

            @block.scalar
            def _(act):
                for g in range(CHUNKS):
                    pos = TC + g if g < TL else g - TL
                    act.wait_ge(gT_full, g + 1)
                    nc.scalar.copy(GR[:, :, pos * P:(pos + 1) * P],
                                   PS[0:4, g, :].rearrange("p (k n) -> p k n", k=4)).then_inc(gT_out, 1)
                act.wait_ge(rows_ok, 1)
                own(act, act_own, act_n, nc.scalar.activation(LF, LF, ACT.Exp))
                nc.scalar.activation(LF, LF, ACT.Ln, bias=const("ones", 4)[:, 0:1]).then_inc(nl_ok, 1)
                act.wait_ge(tt_zero, 1)
                act.wait_ge(rows_ok, 2)
                nc.scalar.copy(TTd[0:4], AR).then_inc(exp_ok, 1)
                nc.scalar.activation(TTd[32:36], W1, ACT.Exp).then_inc(exp_ok, 1)
                nc.scalar.activation(TTd[64:68], W2, ACT.Exp, scale=-1.0).then_inc(exp_ok, 1)
                nc.scalar.activation(TTd[96:100], W3, ACT.Exp, scale=-1.0).then_inc(exp_ok, 1)
                nc.scalar.activation(DPE[:, :], DPE[:, :], ACT.Exp).then_inc(exp_ok, 1)
                act.wait_ge(col_ok, 3)
                for n in range(UNITS):
                    lat, c = chunk_of(n)
                    d = n % 2
                    k_ret, k_ml = (RK[:, c], MK[:, c]) if lat else (RKC[:, c], MKC[:, c])
                    if n in KINDS["state"]:
                        wait(act, r_st, upto_unit("state", n - 1))
                        for h in range(H):
                            ins = nc.scalar.activation(KDB[:, h], k_ret[:, h], ACT.Copy, scale=RDEC[:, 0, 4 * d + h:4 * d + h + 1])
                        ins.then_inc(kd_ok, 1)
                        wait(act, m_st, upto_unit("state", n - 1))
                        for h in range(H):
                            ins = nc.scalar.activation(KWB[:, h], k_ml[:, h], ACT.Copy, scale=COL[:, n, 4 + h:5 + h])
                        ins.then_inc(kw_ok, 1)
                    if not lat:
                        continue
                    act.wait_ge(z_ok, upto_unit("lat", n))
                    nc.scalar.activation(ZE, ZE, ACT.Exp, scale=-1.0).then_inc(e_ok, 1)
                    if n in KINDS["intra"]:
                        act.wait_ge(r_out, upto_unit("intra", n))
                        nc.scalar.copy(OR[:, c], PS[:, 1, :].rearrange("p (h n) -> p h n", h=H)).then_inc(ro_ok, 1)
                    act.wait_ge(m_in, upto_unit("lat", n))
                    wait(act, nd_ok, upto_unit("lat", n - 1))
                    for h in range(H):
                        ins = nc.scalar.activation(TI4[:, h], PS[:, h // 2, (h % 2) * 129:(h % 2) * 129 + 129], ACT.Copy,
                                                   scale=COL[:, n, 8 + h:9 + h])
                    ins.then_inc(ti_ok, 1)

            @block.vector
            def _(dve):
                def o(ins):
                    own(dve, dve_own, dve_n, ins)
                o(nc.vector.memset(MST[:, :, 0:1], 0.0))
                dve.wait_ge(gT_out, CHUNKS)
                dve.wait_ge(ld_gb, 16)
                for d in range(2):
                    o(nc.vector.tensor_scalar(ZF[:, d], GR[:, 2 * d + 1], GB[:, 2 * d + 1:2 * d + 2], None, ALU.add))
                nc.vector.scalar_tensor_tensor(out=LF, in0=ZF, scalar=-1.0, in1=ZF, op0=ALU.mult, op1=ALU.min).then_inc(rows_ok, 1)
                dve.wait_ge(nl_ok, 1)
                o(nc.vector.scalar_tensor_tensor(out=LF, in0=ZF, scalar=0.0, in1=LF, op0=ALU.min, op1=ALU.subtract))

                def row(a, d, pos):
                    lo, hi = pos * P, (pos + 1) * P
                    return a[:, d, lo:hi] if d == 0 else a[:, d, lo:hi][:, ::-1]

                for n in range(UNITS):
                    last = nc.vector.tensor_tensor_scan(row(BB, n % 2, pos_of(n)), const("ones", 4), row(LF, n % 2, pos_of(n)), 0.0,
                                                        op0=ALU.mult, op1=ALU.add)
                o(last)
                for d in range(2):
                    o(nc.vector.scalar_tensor_tensor(out=AR[:, d], in0=GR[:, 2 * d], scalar=GB[:, 2 * d:2 * d + 1], in1=BB[:, d],
                                                     op0=ALU.add, op1=ALU.subtract))
                for s in range(STEPS):
                    for d in range(2):
                        n = 2 * s + d
                        a = row(AR, d, pos_of(n))
                        ins = nc.vector.tensor_tensor_scan(row(AA, d, pos_of(n)), a, a, MST[:, d, s:s + 1], op0=ALU.max, op1=ALU.max)
                    o(ins)
                    for d in range(2):
                        n = 2 * s + d
                        end = pos_of(n) * P + (P - 1 if d == 0 else 0)
                        nc.vector.tensor_tensor(MST[:, d, s + 1:s + 2], BB[:, d, end:end + 1], AA[:, d, end:end + 1], ALU.add)
                        ins = nc.vector.tensor_tensor(DPE[:, n:n + 1], MST[:, d, s:s + 1], AA[:, d, end:end + 1], ALU.subtract)
                    o(ins)
                for n in range(UNITS):
                    s, d = divmod(n, 2)
                    lo = pos_of(n) * P
                    end = lo + (P - 1 if d == 0 else 0)
                    nc.vector.tensor_scalar(W1[:, d, lo:lo + P], AR[:, d, lo:lo + P], AA[:, d, end:end + 1], None, ALU.subtract)
                    nc.vector.tensor_scalar(W2[:, d, lo:lo + P], AA[:, d, lo:lo + P], MST[:, d, s:s + 1], None, ALU.subtract)
                nc.vector.tensor_tensor(W3, BB, AA, ALU.add).then_inc(rows_ok, 1)
                for b in range(3):
                    dve.wait_ge(col_full, b + 1)
                    src = PS[:, b, :].rearrange("p (n q m) -> p n q m", n=4, q=4)[:, :, :, 0:4]
                    dst = COL[:, 4 * b:4 * b + 4, :].rearrange("p n (q m) -> p n q m", q=4)
                    o(nc.vector.tensor_copy(dst, src))
                    nc.vector.tensor_scalar(COL[:, 4 * b:4 * b + 4, 4:8], COL[:, 4 * b:4 * b + 4, 4:8], SCALE, None, ALU.mult).then_inc(col_ok, 1)
                dve.wait_ge(col_ok, 3)
                dve.wait_ge(dpb_full, 1)
                nc.vector.tensor_copy(DPB[:, :, :], PS[:, 3, 0:48].rearrange("p (h n) -> p h n", h=H)).then_inc(dpb_ok, 1)
                dve.wait_ge(dpb_ok, 1)
                for n in range(UNITS):
                    lat, c = chunk_of(n)
                    s, d = divmod(n, 2)
                    neg = const("negf" if d == 0 else "negb")
                    if lat:
                        if n in KINDS["intra"]:
                            dve.wait_ge(r_sc, upto_unit("intra", n))
                            wait(dve, r_out, upto_unit("intra", n - 1))
                            nc.vector.tensor_tensor(PT, PS[:, 0, :].rearrange("p (h n) -> p h n", h=H), DM[:, :, :], ALU.mult).then_inc(pt_ok, 1)
                        dve.wait_ge(m_a, upto_unit("lat", n))
                        wait(dve, pt2_ok, upto_unit("lat", n - 1))
                        for h in range(H):
                            ins = nc.vector.scalar_tensor_tensor(out=ZE[:, h], in0=PS[:, 5, h * P:(h + 1) * P], scalar=COL[:, n, h:h + 1],
                                                                 in1=neg, op0=ALU.subtract, op1=ALU.max)
                        ins.then_inc(z_ok, 1)
                        dve.wait_ge(r_in, upto_unit("lat", n))
                        if n in KINDS["intra"]:
                            dve.wait_ge(ro_ok, upto_unit("intra", n))
                        for h in range(H):
                            ins = nc.vector.scalar_tensor_tensor(out=OR[:, c, h], in0=PS[:, 2, h * P:(h + 1) * P],
                                                                 scalar=RDEC[:, 1, 4 * d + h:4 * d + h + 1], in1=OR[:, c, h],
                                                                 op0=ALU.mult, op1=ALU.add)
                        ins.then_inc(or_ok, 1)
                    if n in KINDS["state"]:
                        dve.wait_ge(r_st, upto_unit("state", n))
                        kv = PS[:, 3, :].rearrange("p (h n) -> p h n", h=H)
                        if lat:
                            dve.wait_ge(r_in, upto_unit("lat", n))
                        if s == 0:
                            ins = nc.vector.tensor_copy(SR[:, d], kv)
                        else:
                            for h in range(H):
                                ins = nc.vector.scalar_tensor_tensor(out=SR[:, d, h], in0=SR[:, d, h], scalar=RDEC[:, 2, 4 * d + h:4 * d + h + 1],
                                                                     in1=kv[:, h], op0=ALU.mult, op1=ALU.add)
                        ins.then_inc(s_ok, 1)
                        wait(dve, s_ok, upto_unit("state", n))
                    if lat:
                        dve.wait_ge(e_ok, upto_unit("lat", n))
                        dve.wait_ge(m_qk, upto_unit("lat", n))
                        wait(dve, m_num, upto_unit("lat", n - 1))
                        nc.vector.scalar_tensor_tensor(out=PT2, in0=PS[:, 4, :].rearrange("p (h n) -> p h n", h=H), scalar=SCALE, in1=ZE,
                                                       op0=ALU.mult, op1=ALU.mult).then_inc(pt2_ok, 1)
                        dve.wait_ge(m_num, upto_unit("lat", n))
                        dve.wait_ge(ti_ok, upto_unit("lat", n))
                        nc.vector.tensor_tensor(ND.rearrange("p (a n) -> p a n", a=2), PS[:, 6:8, 0:258], TI, ALU.add).then_inc(nd_ok, 1)
                        dve.wait_ge(nd_ok, upto_unit("lat", n))
                        o(nc.vector.scalar_tensor_tensor(out=DEN[:, 0:4], in0=ND4[:, :, HD], scalar=-1.0, in1=ND4[:, :, HD],
                                                         op0=ALU.mult, op1=ALU.max))
                        o(nc.vector.tensor_tensor(DEN[:, 0:4], DEN[:, 0:4], COL[:, n, 12:16], ALU.max))
                        o(nc.vector.reciprocal(DEN[:, 4:8], DEN[:, 0:4]))
                        for h in range(H):
                            if n in KINDS["intra"]:
                                ins = nc.vector.tensor_scalar(OM[:, c, h], ND4[:, h, 0:HD], DEN[:, 4 + h:5 + h], None, ALU.mult)
                            else:
                                ins = nc.vector.scalar_tensor_tensor(out=OM[:, c, h], in0=ND4[:, h, 0:HD], scalar=DEN[:, 4 + h:5 + h],
                                                                     in1=OM[:, c, h], op0=ALU.mult, op1=ALU.add)
                        ins.then_inc(om_ok, 1)
                        dve.wait_ge(om_ok, upto_unit("lat", n))
                    if n in KINDS["state"]:
                        dve.wait_ge(m_st, upto_unit("state", n))
                        if lat:
                            dve.wait_ge(m_in, upto_unit("lat", n))
                        kv = PS[:, 4:6, 0:258].rearrange("p a (h n) -> p a h n", h=2)
                        if s == 0:
                            ins = nc.vector.tensor_copy(SM[:, d].rearrange("p (a h) n -> p a h n", a=2), kv)
                        else:
                            for h in range(H):
                                ins = nc.vector.scalar_tensor_tensor(out=SM[:, d, h], in0=SM[:, d, h], scalar=DPB[:, h, n:n + 1],
                                                                     in1=kv[:, h // 2, h % 2], op0=ALU.mult, op1=ALU.add)
                        ins.then_inc(c_ok, 1)
                        dve.wait_ge(c_ok, upto_unit("state", n))

            @block.tensor
            def _(pe):
                for g in range(CHUNKS):
                    for k in range(4):
                        last = nc.tensor.transpose(PS[0:4, g, k * P:(k + 1) * P], GT[:, g, 4 * k:4 * k + 4], ident)
                    last.then_inc(gT_full, 1)
                pe.wait_ge(exp_ok, 5)
                for n in range(UNITS):
                    lo = (n % 2) * (CHUNKS * P) + pos_of(n) * P
                    last = nc.tensor.transpose(PS[:, n // 4, (n % 4) * P:(n % 4 + 1) * P], TT[:, lo:lo + P], ident)
                    if n % 4 == 3:
                        last.then_inc(col_full, 1)
                for h in range(H):
                    last = nc.tensor.matmul(PS[:, 3, h * 12:(h + 1) * 12], sel[0:4, h, :], DPE[:, :], start=True, stop=True)
                last.then_inc(dpb_full, 1)
                pe.wait_ge(dpb_ok, 1)
                for n in range(UNITS):
                    lat, c = chunk_of(n)
                    s, d = divmod(n, 2)
                    cs = slice(c * P, (c + 1) * P)
                    v_ret, v_ml = (RV[:, c], MV[:, c]) if lat else (RVC[:, c], MVC[:, c])
                    if lat:
                        if n in KINDS["intra"]:
                            wait(pe, ti_ok, upto_unit("lat", n - 1))
                            for h in range(H):
                                last = nc.tensor.matmul(PS[:, 0, h * P:(h + 1) * P], RKT[:, h, cs], RQT[:, h, cs], start=True, stop=True)
                            last.then_inc(r_sc, 1)
                        wait(pe, c_ok, upto_unit("state", n - 1))
                        wait(pe, pt2_ok, upto_unit("lat", n - 1))
                        lo = pos_of(n) * P
                        for h in range(H):
                            last = nc.tensor.matmul(PS[:, 5, h * P:(h + 1) * P], sel[0:4, h, :], AA[:, d, lo:lo + P], start=True, stop=True)
                        last.then_inc(m_a, 1)
                        for h in range(H):
                            last = nc.tensor.matmul(PS[:, 4, h * P:(h + 1) * P], MKT[:, h, cs], MQT[:, h, cs], start=True, stop=True)
                        last.then_inc(m_qk, 1)
                        wait(pe, or_ok, upto_unit("lat", n - 1))
                        wait(pe, s_ok, upto_unit("state", n - 2))
                        for h in range(H):
                            last = nc.tensor.matmul(PS[:, 2, h * P:(h + 1) * P], RQT[:, h, cs], SR[:, d, h], start=True, stop=True)
                        last.then_inc(r_in, 1)
                        if n in KINDS["intra"]:
                            pe.wait_ge(pt_ok, upto_unit("intra", n))
                            for h in range(H):
                                last = nc.tensor.matmul(PS[:, 1, h * P:(h + 1) * P], PT[:, h], v_ret[:, h], start=True, stop=True)
                            last.then_inc(r_out, 1)
                    if n in KINDS["state"]:
                        pe.wait_ge(kd_ok, upto_unit("state", n))
                        wait(pe, s_ok, upto_unit("state", n - 1))
                        for h in range(H):
                            last = nc.tensor.matmul(PS[:, 3, h * P:(h + 1) * P], KDB[:, h], v_ret[:, h], start=True, stop=True)
                        last.then_inc(r_st, 1)
                    if lat:
                        wait(pe, c_ok, upto_unit("state", n - 2))
                        if n in KINDS["intra"]:
                            pe.wait_ge(ro_ok, upto_unit("intra", n))
                        wait(pe, ti_ok, upto_unit("lat", n - 1))
                        for h in range(H):
                            last = nc.tensor.matmul(PS[:, h // 2, (h % 2) * 129:(h % 2) * 129 + 129], MQT[:, h, cs], SM[:, d, h], start=True, stop=True)
                        last.then_inc(m_in, 1)
                        pe.wait_ge(pt2_ok, upto_unit("lat", n))
                        wait(pe, nd_ok, upto_unit("lat", n - 1))
                        for h in range(H):
                            last = nc.tensor.matmul(PS[:, 6 + h // 2, (h % 2) * 129:(h % 2) * 129 + 129], PT2[:, h], v_ml[:, h], start=True, stop=True)
                        last.then_inc(m_num, 1)
                    if n in KINDS["state"]:
                        pe.wait_ge(kw_ok, upto_unit("state", n))
                        wait(pe, c_ok, upto_unit("state", n - 1))
                        for h in range(H):
                            last = nc.tensor.matmul(PS[:, 4 + h // 2, (h % 2) * 129:(h % 2) * 129 + 129], KWB[:, h], v_ml[:, h], start=True, stop=True)
                        last.then_inc(m_st, 1)
        if upto == 2:
            return

        WO = ring(0, 8192).rearrange("p (k n) -> p k n", k=KD)
        WR = ring(8192, 512).rearrange("p (k n) -> p k n", k=KD)
        RB = ring(8704, NE)
        SHG = pr(0, 2048).rearrange("p (k n) -> p k n", k=KD)
        SHU = pr(2048, 2048).rearrange("p (k n) -> p k n", k=KD)
        SHD = pr(4096, 2048).rearrange("p (c n) -> p c n", c=2)
        HT2 = pr(6144, 4096).rearrange("p (k n) -> p k n", k=KD)
        BC = pr(10240, 4096).rearrange("p (m n) -> p m n", m=4)
        YN = pr(14336, 1024)
        YT = pr(15360, 1024).rearrange("p (k n) -> p k n", k=KD)
        TB = pr(16384, 1024)
        HP = pr(17408, 2048).rearrange("p (b n) -> p b n", b=2)
        GAIN = pr(19456, 1024)
        FOLD = [ring(8768, 1024), ring(9792, 1024), ring(10816, 1024), ring(16384, 1024), ring(17408, 1024), ST[:, 0:1024], ST[:, 1024:2048]]
        SHS = ST[:, 0:512].rearrange("p (b n) -> p b n", b=2)
        SHH = ST[:, 512:1024].rearrange("p (b n) -> p b n", b=2)
        SHT = ST[:, 1024:1536].rearrange("p (b c n) -> p b c n", b=2, c=2)
        SHY = pr(14336, 2048).rearrange("p (b n) -> p b n", b=2)
        ZERO = pr(16384, 1024)
        RWL = pr(22520, 2080).rearrange("p (t l c w) -> p t l c w", t=TL, l=LEVELS, w=2)
        RWLc = pr(22520, 2080).rearrange("p (t c w) -> p t c w", t=TL, w=2)
        BNS = ring(11840, 48).rearrange("p (j n) -> p j n", n=6)
        MVR = ring(11888, 16).rearrange("p (j n) -> p j n", n=2)
        R2 = ring(11904, 4 * TL).rearrange("p (t n) -> p t n", n=4)
        def rt(a, n):
            return pr(20504 + a, n)
        SC = rt(0, 256).rearrange("p (t e) -> p t e", t=TL)
        SEL = rt(256, 64)
        SELM = rt(320, 64)
        REP = rt(384, 64)
        MSK = rt(448, 256).rearrange("p (t e) -> p t e", t=TL)
        WGT = rt(704, 256).rearrange("p (t e) -> p t e", t=TL)
        M8 = rt(960, 64)
        GRP = rt(1024, 12)
        G8 = rt(1036, 12)
        GRR = rt(1048, 12)
        GMK = rt(1060, 8)
        GNEG = rt(1068, 8)
        T8 = rt(1076, 8)
        WS = rt(1084, 2)
        CNT = rt(1090, 4)
        PEND = rt(1096, 1)
        CMP = rt(1100, LIST)
        JST = rt(1220, 2 * LIST + 1)
        BLF = PR[0:1, 22000:22000 + 2 * LIST].rearrange("p (a n) -> p a n", a=2)

        ld_wo, ld_wr, ld_sh, ld_bc, ld_fold, ld_gain, ld_rb = (sem("ld_" + n) for n in ("wo", "wr", "sh", "bc", "fold", "gain", "rb"))
        gated, bn_ok, sd_ok, yn_ok, yT_full, yT_out, z_full, z_out, sq_ok, x1_ok, sq2_ok, hp_ok, h_st, h_st2, hT_full, hT_out = (sem("c_" + n) for n in (
            "gated", "bn", "sd", "yn", "yTf", "yTo", "zf", "zo", "sq", "x1", "sq2", "hp", "hst", "hst2", "hTf", "hTo"))
        r_full, sc_ok, sg_full, su_full, ss_silu, hid_ok, sT_full, sT_out, sd_full, sd_out, y_st, zero_ok = (sem("c_" + n) for n in (
            "rf", "sc", "sgf", "suf", "silu", "hid", "sTf", "sTo", "sdf", "sdo", "yst", "zero"))
        y_st2 = sem("c_yst2")
        sc_done = sem("sc_done")
        msk_ok, rank_full, cnt_full, cmp_in, cmp_ok, list_full, pend_full, bl_ok = (sem("c_" + n) for n in (
            "msk", "rankf", "cntf", "cmpin", "cmp", "listf", "pendf", "bl"))
        h_st_s, y_st_s = [h_st, h_st2], [y_st, y_st2]

        def router_tile(dve, o, i):
            sc3 = SEL.rearrange("p (g e) -> p g e", g=NG)
            o(nc.vector.tensor_tensor(SEL, SC[:, i], RB, ALU.add))
            for g in range(NG):
                last = nc.vector.max(M8[:, g * 8:(g + 1) * 8], SEL[:, g * 8:(g + 1) * 8])
            o(last)
            m8 = M8.rearrange("p (g e) -> p g e", g=NG)
            o(nc.vector.tensor_tensor(GRP[:, 0:8], m8[:, :, 0], m8[:, :, 1], ALU.add))
            o(nc.vector.max(G8[:, 0:8], GRP[:, 0:8]))
            o(nc.vector.memset(G8[:, 4:8], -BIG))
            o(nc.vector.match_replace(out=GRR, in_to_replace=G8[:, 0:8], in_values=GRP, imm_value=-2 * BIG))
            o(nc.vector.tensor_tensor(GMK, GRR[:, 0:8], GRP[:, 0:8], ALU.not_equal))
            o(nc.vector.tensor_scalar(GNEG, GMK, 1.0, BIG, ALU.subtract, ALU.mult))
            gm = GMK.unsqueeze(2).to_broadcast([P, NG, 8])
            gn = GNEG.unsqueeze(2).to_broadcast([P, NG, 8])
            sm = SELM.rearrange("p (g e) -> p g e", g=NG)
            o(nc.vector.tensor_tensor(sm, sc3, gm, ALU.mult))
            o(nc.vector.tensor_tensor(sm, sm, gn, ALU.add))
            o(nc.vector.max(T8, SELM))
            o(nc.vector.match_replace(out=REP, in_to_replace=T8, in_values=SELM, imm_value=-2 * BIG))
            nc.vector.tensor_tensor(MSK[:, i], REP, SELM, ALU.not_equal).then_inc(msk_ok, 1)
            dve.wait_ge(msk_ok, i + 1)
            o(nc.vector.tensor_tensor(WGT[:, i], SC[:, i], MSK[:, i], ALU.mult))
            o(nc.vector.reduce_sum(WS[:, 0:1], WGT[:, i], AX.X))
            o(nc.vector.reciprocal(WS[:, 1:2], WS[:, 0:1]))
            o(nc.vector.tensor_scalar(WGT[:, i], WGT[:, i], WS[:, 1:2], ROUTED_SCALE, ALU.mult, ALU.mult))

        with nc.Block() as block:
            @block.sync
            def _(sp):
                sp.dma_start(GAIN[:, 0:W], t["ret_norm_g"][0].partition_broadcast(P)).then_inc(ld_gain, 16)
                sp.dma_start(GAIN[:, W:2 * W], t["mlstm_norm_g"][0].partition_broadcast(P)).then_inc(ld_gain, 16)
                sp.dma_start(WO, t["w_out"][0].rearrange("(k p) n -> p k n", p=P)).then_inc(ld_wo, 16)
                for m in range(4):
                    sp.dma_start(BC[:, m], m_dram[m].partition_broadcast(P)).then_inc(ld_bc, 16)
                for dst, src in zip(FOLD, [t["b_mod"][0, (2 + m) * D:(3 + m) * D] for m in range(4)] + [t["norm_g"][0, m] for m in (1, 2, 3)]):
                    sp.dma_start(dst, src.partition_broadcast(P)).then_inc(ld_fold, 16)
                sp.dma_start(WR, t["w_router"][0].rearrange("(p k) n -> p k n", k=KD)).then_inc(ld_wr, 16)
                sp.dma_start(RB, t["router_bias"][0].partition_broadcast(P)).then_inc(ld_rb, 16)
                sp.dma_start(SHG, t["ws_gate"][0].rearrange("(p k) n -> p k n", k=KD)).then_inc(ld_sh, 16)
                sp.dma_start(SHU, t["ws_up"][0].rearrange("(p k) n -> p k n", k=KD)).then_inc(ld_sh, 16)
                sp.dma_start(SHD, t["ws_down"][0].rearrange("(p c) n -> p c n", c=2)).then_inc(ld_sh, 16)
                for i in range(TL):
                    sp.wait_ge(hp_ok, i + 1)
                    sp.dma_start(h_dram[i * P:(i + 1) * P, :], HP[:, i % 2]).then_inc(h_st_s[i % 2], 16)
                for i in range(TL):
                    sp.wait_ge(sd_out, 2 * i + 2)
                    sp.dma_start(y_dram[i * P:(i + 1) * P, :], SHY[:, i % 2]).then_inc(y_st_s[i % 2], 16)
                for s in h_st_s + y_st_s:
                    sp.wait_ge(s, 16 * TL // 2)

            @block.gpsimd
            def _(pool):
                pool.wait_ge(ld_gain, 32)
                for i in range(TL):
                    nc.gpsimd.tensor_tensor(RG[:, i], RG[:, i], GAIN[:, 0:W], ALU.mult)
                    nc.gpsimd.tensor_tensor(MO[:, i], MO[:, i], GAIN[:, W:2 * W], ALU.mult).then_inc(gated, 1)
                pool.wait_ge(zero_ok, 1)
                pool.dma_start(y_dram[TRASH:TRASH + P, :], ZERO).then_inc(sc_done, 16)
                pool.wait_ge(sc_done, 16)

            @block.scalar
            def _(act):
                def norm_std(i, dst, src_ss):
                    return nc.scalar.activation(dst, src_ss, ACT.Sqrt, bias=const("eps"), scale=1.0 / D)

                def mixed(i):
                    act.wait_ge(bn_ok, i + 1)
                    nc.scalar.activation(MVR[:, :, 1], MVR[:, :, 1], ACT.Sqrt, bias=const("eps")).then_inc(sd_ok, 1)
                    act.wait_ge(yT_full, i + 1)
                    if i:
                        act.wait_ge(z_full, i)
                    nc.scalar.copy(YT.rearrange("p (b k) n -> p b (k n)", b=2), PS[:, 0:2, :]).then_inc(yT_out, 1)

                def residual(i):
                    act.wait_ge(z_full, i + 1)
                    nc.scalar.activation(TB.rearrange("p (b n) -> p b n", b=2), PS[:, 2:4, :], ACT.Square, accum_out=R2[:, i, 0:1]).then_inc(sq_ok, 1)
                    act.wait_ge(sq_ok, i + 1)
                    norm_std(i, R2[:, i, 1:2], R2[:, i, 0:1]).then_inc(z_out, 1)
                    act.wait_ge(x1_ok, i + 1)
                    own(act, act_own, act_n, nc.scalar.activation(TB, X[:, i], ACT.Square, accum_out=R2[:, i, 2:3]))
                    norm_std(i, R2[:, i, 3:4], R2[:, i, 2:3]).then_inc(sq2_ok, 1)
                    act.wait_ge(hT_full, i + 1)
                    nc.scalar.copy(HT2[:, :, i * P:(i + 1) * P], PS[:, 4:6, :].rearrange("p b (k n) -> p (b k) n", n=P)).then_inc(hT_out, 1)

                mixed(0)
                for i in range(1, TL):
                    mixed(i)
                    residual(i - 1)
                residual(TL - 1)
                act.wait_ge(r_full, TL)
                nc.scalar.activation(SC, PS[:, 6, 0:TL * NE].rearrange("p (t e) -> p t e", t=TL), ACT.Sigmoid).then_inc(sc_ok, 1)
                for i in range(TL):
                    act.wait_ge(sg_full, i + 1)
                    if i >= 2:
                        act.wait_ge(hid_ok, i - 1)
                    nc.scalar.activation(SHS[:, i % 2], PS[:, 0, 0:FF], ACT.Silu).then_inc(ss_silu, 1)
                    act.wait_ge(sT_full, i + 1)
                    nc.scalar.copy(SHT[:, i % 2], PS[:, 4, 0:FF].rearrange("p (c n) -> p c n", c=2)).then_inc(sT_out, 1)
                    act.wait_ge(sd_full, i + 1)
                    if i >= 2:
                        act.wait_ge(y_st_s[i % 2], 16 * (i // 2))
                    nc.scalar.copy(SHY[:, i % 2, 0:512], PS[:, 2, :]).then_inc(sd_out, 1)
                    nc.scalar.copy(SHY[:, i % 2, 512:1024], PS[:, 3, :]).then_inc(sd_out, 1)

            @block.vector
            def _(dve):
                def o(ins):
                    own(dve, dve_own, dve_n, ins)

                def head_norms(i):
                    if i:
                        dve.wait_ge(yT_full, i)
                    for m, src in enumerate((OR, OM)):
                        for h in range(H):
                            last = nc.vector.bn_stats(BNS[:, m * H + h, :], src[:, i, h])
                    o(last)
                    for j in range(8):
                        last = nc.vector.bn_aggr(MVR[:, j, :], BNS[:, j, :])
                    last.then_inc(bn_ok, 1)
                    dve.wait_ge(sd_ok, i + 1)
                    o(nc.vector.reciprocal(MVR[:, :, 1], MVR[:, :, 1]))
                    for m, src in enumerate((OR, OM)):
                        for h in range(H):
                            j = m * H + h
                            last = nc.vector.tensor_scalar(YN[:, j * HD:(j + 1) * HD], src[:, i, h], MVR[:, j, 0:1], MVR[:, j, 1:2],
                                                           ALU.subtract, ALU.mult)
                    o(last)
                    dve.wait_ge(gated, i + 1)
                    nc.vector.tensor_tensor(YN[:, 0:W], YN[:, 0:W], RG[:, i], ALU.mult)
                    nc.vector.tensor_tensor(YN[:, W:2 * W], YN[:, W:2 * W], MO[:, i], ALU.mult).then_inc(yn_ok, 1)

                def residual(i):
                    dve.wait_ge(z_out, i + 1)
                    o(nc.vector.reciprocal(R2[:, i, 1:2], R2[:, i, 1:2]))
                    o(nc.vector.scalar_tensor_tensor(out=TB.rearrange("p (b n) -> p b n", b=2), in0=PS[:, 2:4, :], scalar=R2[:, i, 1:2],
                                                     in1=BC[:, 0].rearrange("p (b n) -> p b n", b=2), op0=ALU.mult, op1=ALU.mult))
                    nc.vector.tensor_tensor(X[:, i], X[:, i], TB, ALU.add).then_inc(x1_ok, 1)
                    dve.wait_ge(sq2_ok, i + 1)
                    o(nc.vector.reciprocal(R2[:, i, 3:4], R2[:, i, 3:4]))
                    o(nc.vector.scalar_tensor_tensor(out=TB, in0=X[:, i], scalar=R2[:, i, 3:4], in1=BC[:, 2], op0=ALU.mult, op1=ALU.mult))
                    if i >= 2:
                        dve.wait_ge(h_st_s[i % 2], 16 * (i // 2))
                        dve.wait_ge(hT_full, i - 1)
                    nc.vector.tensor_tensor(HP[:, i % 2].rearrange("q (k p) -> q p k", k=KD), TB.rearrange("q (p k) -> q p k", k=KD),
                                            BC[:, 1].rearrange("q (p k) -> q p k", k=KD), ALU.add).then_inc(hp_ok, 1)
                    dve.wait_ge(hp_ok, i + 1)

                head_norms(0)
                head_norms(1)
                dve.wait_ge(ld_bc, 64)
                dve.wait_ge(ld_fold, 16 * 7)
                for m in range(4):
                    last = nc.vector.tensor_tensor(BC[:, m], BC[:, m], FOLD[m], ALU.add)
                o(last)
                nc.vector.tensor_tensor(BC[:, 0], BC[:, 0], FOLD[4], ALU.mult)
                nc.vector.scalar_tensor_tensor(out=BC[:, 2], in0=BC[:, 2], scalar=1.0, in1=FOLD[5], op0=ALU.add, op1=ALU.mult)
                o(nc.vector.tensor_tensor(BC[:, 3], BC[:, 3], FOLD[6], ALU.mult))
                residual(0)
                head_norms(2)
                residual(1)
                head_norms(3)
                residual(2)
                residual(3)
                dve.wait_ge(yT_full, TL)
                nc.vector.memset(ZERO, 0.0).then_inc(zero_ok, 1)
                nc.vector.memset(GRP[:, 8:12], -BIG)
                o(nc.vector.memset(RWL, -1.0))
                dve.wait_ge(sc_ok, 1)
                dve.wait_ge(ld_rb, 16)
                for i in range(TL):
                    dve.wait_ge(su_full, i + 1)
                    dve.wait_ge(ss_silu, i + 1)
                    if i >= 2:
                        dve.wait_ge(sT_full, i - 1)
                    nc.vector.tensor_tensor(SHH[:, i % 2].rearrange("p (c n) -> p n c", c=2), SHS[:, i % 2].rearrange("p (n c) -> p n c", c=2),
                                            PS[:, 1, 0:FF].rearrange("p (n c) -> p n c", c=2), ALU.mult).then_inc(hid_ok, 1)
                    router_tile(dve, o, i)
                dve.wait_ge(rank_full, 1)
                rank = PS[:, 6, 256:512].rearrange("p (t e) -> p t e", t=TL)
                rk1 = SC
                o(nc.vector.scalar_tensor_tensor(out=rk1, in0=rank, scalar=1.0, in1=MSK, op0=ALU.add, op1=ALU.mult))
                for l in range(LEVELS):
                    nc.vector.tensor_scalar(RWL[:, :, l, 0:NE, 0], rk1, 1.0 + l * P, None, ALU.subtract)
                    last = nc.vector.tensor_copy(RWL[:, :, l, 0:NE, 1], WGT)
                o(last)
                dve.wait_ge(cnt_full, 1)
                cnt = PS[0:NE, 7, 0:1]
                o(nc.vector.tensor_scalar(CNT[0:NE, 0:1], cnt, 0.0, None, ALU.is_gt))
                for l in range(1, LEVELS):
                    nc.vector.scalar_tensor_tensor(out=CNT[0:NE, 0:1], in0=cnt, scalar=float(l * P), in1=CNT[0:NE, 0:1],
                                                   op0=ALU.is_gt, op1=ALU.add).then_inc(cmp_in, 1)
                    dve.wait_ge(cmp_in, l)
                dve.wait_ge(pend_full, 1)
                o(nc.vector.tensor_copy(PEND[0:NE], PS[0:NE, 7, 1:2]))
                nc.vector.tensor_scalar(CMP[0:NE, :], const("iota", NE)[:, 0:LIST], PEND[0:NE], None, ALU.is_ge).then_inc(cmp_ok, 1)
                dve.wait_ge(list_full, 1)
                o(nc.vector.tensor_copy(JST[0:1, :], PS[0:1, 7, 2:2 + 2 * LIST + 1]))
                e_j, st_j = JST[0:1, 0:LIST], JST[0:1, LIST:2 * LIST]
                o(nc.vector.tensor_tensor(st_j, const("iota", 1)[:, 0:LIST], st_j, ALU.subtract))
                o(nc.vector.tensor_scalar(st_j, st_j, float(LEVELS - 1), float(CODES), ALU.min, ALU.mult))
                o(nc.vector.tensor_tensor(BLF[:, 0, :], st_j, e_j, ALU.add))
                o(nc.vector.tensor_scalar(BLF[:, 1, :], e_j, float(NE - 1), None, ALU.min))
                o(nc.vector.tensor_copy(BLI[:, 0:2 * LIST], BLF[:, :, :].rearrange("p a n -> p (a n)")))
                total = JST[0:1, 2 * LIST:2 * LIST + 1]
                o(nc.vector.tensor_scalar(BLF[:, 0, 0:ITERS], const("iota", 1)[:, 0:ITERS], float(U), total, ALU.mult, ALU.is_lt))
                o(nc.vector.reduce_sum(BLF[:, 1, 0:1], BLF[:, 0, 0:ITERS], AX.X))
                nc.vector.tensor_copy(BLI[:, 2 * LIST:2 * LIST + 1], BLF[:, 1, 0:1]).then_inc(bl_ok, 1)
                dve.wait_ge(bl_ok, 1)
                for u in range(U):
                    nc.vector.tensor_copy(RHS[:, u, :, 2], const("tok1"))

            @block.tensor
            def _(pe):
                def transpose_y(i):
                    pe.wait_ge(yn_ok, i + 1)
                    if i:
                        pe.wait_ge(yT_out, i)
                    for k in range(KD):
                        last = nc.tensor.transpose(PS[:, k // 4, (k % 4) * P:(k % 4 + 1) * P], YN[:, k * P:(k + 1) * P], ident)
                    last.then_inc(yT_full, 1)

                def project_y(i):
                    pe.wait_ge(yT_out, i + 1)
                    pe.wait_ge(ld_wo, 16)
                    if i:
                        pe.wait_ge(x1_ok, i)
                    for half in range(2):
                        for k in range(KD):
                            last = nc.tensor.matmul(PS[:, 2 + half, :], YT[:, k, :], WO[:, k, half * 512:(half + 1) * 512], start=k == 0, stop=k == KD - 1)
                    last.then_inc(z_full, 1)

                def transpose_h(i):
                    pe.wait_ge(hp_ok, i + 1)
                    if i:
                        pe.wait_ge(hT_out, i)
                    for k in range(KD):
                        last = nc.tensor.transpose(PS[:, 4 + k // 4, (k % 4) * P:(k % 4 + 1) * P], HP[:, i % 2, k * P:(k + 1) * P], ident)
                    last.then_inc(hT_full, 1)

                def router(i):
                    pe.wait_ge(hT_out, i + 1)
                    pe.wait_ge(ld_wr, 16)
                    for k in range(KD):
                        last = nc.tensor.matmul(PS[:, 6, i * NE:(i + 1) * NE], HT2[:, k, i * P:(i + 1) * P], WR[:, k, :], start=k == 0, stop=k == KD - 1)
                    last.then_inc(r_full, 1)

                def shared(i):
                    pe.wait_ge(hT_out, i + 1)
                    pe.wait_ge(ld_sh, 48)
                    if i == 0:
                        pe.wait_ge(yT_out, TL)
                    else:
                        pe.wait_ge(hid_ok, i)
                    for bank, w, done in ((0, SHG, sg_full), (1, SHU, su_full)):
                        for k in range(KD):
                            last = nc.tensor.matmul(PS[:, bank, 0:FF], HT2[:, k, i * P:(i + 1) * P], w[:, k, :], start=k == 0, stop=k == KD - 1)
                        last.then_inc(done, 1)

                def shared_down(i):
                    pe.wait_ge(hid_ok, i + 1)
                    if i == 0:
                        pe.wait_ge(hT_out, TL)
                        pe.wait_ge(x1_ok, TL)
                    else:
                        pe.wait_ge(sT_out, i)
                        pe.wait_ge(sd_out, 2 * i)
                    for c in range(2):
                        last = nc.tensor.transpose(PS[:, 4, c * P:(c + 1) * P], SHH[:, i % 2, c * P:(c + 1) * P], ident)
                    last.then_inc(sT_full, 1)
                    pe.wait_ge(sT_out, i + 1)
                    for half in range(2):
                        for c in range(2):
                            last = nc.tensor.matmul(PS[:, 2 + half, :], SHT[:, i % 2, c, :], SHD[:, c, half * 512:(half + 1) * 512], start=c == 0, stop=c == 1)
                    last.then_inc(sd_full, 1)

                transpose_y(0)
                project_y(0)
                for i in range(1, TL):
                    if i > 1:
                        transpose_h(i - 2)
                        router(i - 2)
                    transpose_y(i)
                    project_y(i)
                transpose_h(2)
                router(2)
                transpose_h(3)
                router(3)
                for i in range(TL):
                    shared(i)
                    shared_down(i)
                pe.wait_ge(msk_ok, TL)
                for i in range(TL):
                    out_i = PS[:, 6, 256 + i * NE:256 + (i + 1) * NE]
                    for j in range(i + 1):
                        last = nc.tensor.matmul(out_i, const("lt" if j == i else "ones"), MSK[:, j], start=j == 0, stop=j == i)
                last.then_inc(rank_full, 1)
                for i in range(TL):
                    last = nc.tensor.matmul(PS[0:NE, 7, 0:1], MSK[:, i], const("ones")[:, 0:1], start=i == 0, stop=i == TL - 1)
                last.then_inc(cnt_full, 1)
                pe.wait_ge(cmp_in, LEVELS - 1)
                nc.tensor.matmul(PS[0:NE, 7, 1:2], const("le", NE)[:, 0:NE], CNT[0:NE, 0:1], start=True, stop=True).then_inc(pend_full, 1)
                pe.wait_ge(cmp_ok, 1)
                nc.tensor.matmul(PS[0:1, 7, 2:2 + LIST], const("ones", NE)[:, 0:1], CMP[0:NE, :], start=True, stop=True)
                nc.tensor.matmul(PS[0:1, 7, 2 + LIST:2 + 2 * LIST], CNT[0:NE, 0:1], CMP[0:NE, :], start=True, stop=True)
                nc.tensor.matmul(PS[0:1, 7, 2 + 2 * LIST:3 + 2 * LIST], CNT[0:NE, 0:1], const("ones", NE)[:, 0:1], start=True, stop=True).then_inc(list_full, 1)
        if upto == 3:
            return

        XB = pr(0, 1024 * U).rearrange("p (u n) -> p u n", u=U)
        XBT = pr(3072, 1024 * U).rearrange("p (u k n) -> p u k n", u=U, k=KD)
        YB = pr(6144, 1024 * U).rearrange("p (u n) -> p u n", u=U)
        OH = pr(9216, 512).rearrange("p (t n) -> p t n", t=TL)
        SG = pr(14336, FF * U).rearrange("p (u n) -> p u n", u=U)
        HB = pr(15104, FF * U).rearrange("p (u n) -> p u n", u=U)
        HBT = pr(15872, FF * U).rearrange("p (u c n) -> p u c n", u=U, c=2)
        EQ = pr(16640, U)
        EG = [ring(u * 6144, 2048).rearrange("p (k n) -> p k n", k=KD) for u in range(U)]
        EU = [ring(u * 6144 + 2048, 2048).rearrange("p (k n) -> p k n", k=KD) for u in range(U)]
        ED = [ring(u * 6144 + 4096, 2048).rearrange("p (c n) -> p c n", c=2) for u in range(U)]
        weights = [("w_gate", 0, "e (p k) n -> e p (k n)", KD), ("w_up", 2048, "e (p k) n -> e p (k n)", KD),
                   ("w_down", 4096, "e (p k) n -> e p (k n)", 2)]
        w_src = [t[name][0].rearrange(how, k=k) for name, _, how, k in weights]

        w_ld = [[sem(f"{name}_ld{u}") for u in range(U)] for name, *_ in weights]
        x_ld = [sem(f"x_ld{u}") for u in range(U)]
        used = [[sem(f"{name}_used{u}") for u in range(U)] for name, *_ in weights[:2]]
        rhs_ok, oh_ok, idx_full, eq_ok, idx_ok, xT_full, xT_out = (sem("e_" + n) for n in (
            "rhs", "oh", "idxf", "eq", "idx", "xTf", "xTo"))
        silu2_ok, hid2_ok, h2T_full, h2T_out, y_full, y_act, y_dve = (sem("e_" + n) for n in (
            "silu", "hid", "hTf", "hTo", "yf", "yact", "ydve"))

        gather_go, scatter_go = sem("gather_go"), sem("scatter_go")

        def rounds(eng):
            return eng.snap(eng.value_load(BLI[0:1, 2 * LIST:2 * LIST + 1], min_val=1, max_val=ITERS))

        with nc.Block() as block:
            @block.sync
            def _(sp):
                def load(j, u):
                    e = sp.value_load(BLI[0:1, bass.ds(j + LIST, 1)], min_val=0, max_val=NE - 1)
                    for m, (_, at0, _, _) in enumerate(weights):
                        yield m
                        sp.dma_start(ring(u * 6144 + at0, 2048), w_src[m][bass.ds(e, 1)].rearrange("e p n -> (e p) n")).then_inc(w_ld[m][u], 16)
                for u in range(U):
                    for _ in load(u, u):
                        pass
                n_rounds = rounds(sp)
                with sp.Fori(0, ITERS - 1) as i:
                    with sp.If(i + 1 < n_rounds):
                        for u in range(U):
                            for m in load(i * U + (U + u), u):
                                if m < 2:
                                    sp.wait_ge(used[m][u], i + 1)
                                else:
                                    sp.wait_ge(y_full, i * U + (u + 1))

            @block.gpsimd
            def _(pool):
                def gather(u, v):
                    pool.wait_ge(idx_ok, v)
                    pool.sem_inc(gather_go, 1)
                    nc.gpsimd.indirect_dma_start(
                        out=XB[:, u], out_offset=None, in_=h_dram,
                        in_offset=bass.IndirectOffsetOnAxis(ap=IDX[:, u, 0:1], axis=0)).then_inc(x_ld[u], 16)
                gather(0, 1)
                gather(1, 2)
                n_rounds = rounds(pool)
                with pool.Fori(0, ITERS) as i:
                    with pool.If(i < n_rounds):
                        for u in range(U):
                            pool.wait_ge(xT_full, i * U + (u + 1))
                            gather((u + 2) % U, i * U + (u + 3))
                            pool.wait_ge(y_act, i * U + (u + 1))
                            pool.wait_ge(y_dve, i * U + (u + 1))
                            pool.wait_ge(sc_done, i * (16 * U) + 16 * (u + 1))
                            pool.sem_inc(scatter_go, 1)
                            nc.gpsimd.indirect_dma_start(
                                out=y_dram, out_offset=bass.IndirectOffsetOnAxis(ap=IDX[:, u, 1:2], axis=0),
                                in_=YB[:, u], in_offset=None, compute_op=ALU.add).then_inc(sc_done, 16)
                pool.wait_ge(sc_done, n_rounds * (16 * U) + 16)
                pool.wait_ge(x_ld[1], n_rounds * 16 + 16)

            @block.scalar
            def _(act):
                def xT_evacuate(u, v):
                    act.wait_ge(xT_full, v)
                    for half in range(2):
                        ins = nc.scalar.copy(XBT[:, u, half * 4:half * 4 + 4, :], PS[:, 2 + half, :].rearrange("p (k n) -> p k n", k=4))
                    ins.then_inc(xT_out, 1)
                xT_evacuate(0, 1)
                n_rounds = rounds(act)
                with act.Fori(0, ITERS) as i:
                    with act.If(i < n_rounds):
                        for u in range(U):
                            act.wait_ge(used[0][u], i + 1)
                            nc.scalar.activation(SG[:, u], PS[:, 0, 0:FF], ACT.Silu).then_inc(silu2_ok, 1)
                            xT_evacuate((u + 1) % U, i * U + (u + 2))
                            act.wait_ge(y_full, i * U + (u + 1))
                            nc.scalar.copy(YB[:, u, 0:512], PS[:, 6, :]).then_inc(y_act, 1)

            @block.vector
            def _(dve):
                def one_hot(code_at, u, v):
                    code = dve.value_load(BLI[0:1, bass.ds(code_at, 1)], min_val=0, max_val=CODES * LEVELS - 1)
                    nc.vector.tensor_copy(RHS[:, u, :, 0:2], RWLc[:, :, bass.ds(code, 1), :].rearrange("p t c w -> p t (c w)")).then_inc(rhs_ok, 1)
                    dve.wait_ge(rhs_ok, v)
                    for c in range(TL):
                        ins = nc.vector.tensor_scalar(OH[:, c], const("iota"), RHS[:, u, c, 0:1], None, ALU.is_equal)
                    ins.then_inc(oh_ok, 1)

                def indices(u, v):
                    dve.wait_ge(idx_full, v)
                    nc.vector.tensor_scalar(IDX[:, u, 0:1], PS[:, 5, 1:2], 1.0, 0.0, ALU.subtract, ALU.max)
                    nc.vector.tensor_copy(WCOL[:, u], PS[:, 5, 0:1])
                    nc.vector.tensor_scalar(EQ[:, u:u + 1], PS[:, 5, 1:2], 0.0, const("trash"), ALU.is_equal, ALU.mult).then_inc(eq_ok, 1)
                    dve.wait_ge(eq_ok, v)
                    nc.vector.tensor_scalar(IDX[:, u, 1:2], PS[:, 5, 1:2], 1.0, EQ[:, u:u + 1], ALU.subtract, ALU.add).then_inc(idx_ok, 1)

                one_hot(0, 0, 1)
                indices(0, 1)
                one_hot(1, 1, 2)
                indices(1, 2)
                n_rounds = rounds(dve)
                with dve.Fori(0, ITERS) as i:
                    with dve.If(i < n_rounds):
                        for u in range(U):
                            ahead = (u + 2) % U
                            one_hot(i * U + (u + 2), ahead, i * U + (u + 3))
                            dve.wait_ge(silu2_ok, i * U + (u + 1))
                            dve.wait_ge(used[1][u], i + 1)
                            nc.vector.scalar_tensor_tensor(
                                out=HB[:, u].rearrange("p (c n) -> p n c", c=2), in0=SG[:, u].rearrange("p (n c) -> p n c", c=2), scalar=WCOL[:, u],
                                in1=PS[:, 1, 0:FF].rearrange("p (n c) -> p n c", c=2), op0=ALU.mult, op1=ALU.mult).then_inc(hid2_ok, 1)
                            dve.wait_ge(h2T_full, i * U + (u + 1))
                            nc.vector.tensor_copy(HBT[:, u], PS[:, 4, 0:FF].rearrange("p (c n) -> p c n", c=2)).then_inc(h2T_out, 1)
                            dve.wait_ge(sc_done, i * (16 * U) + 16 * (u + 1))
                            indices(ahead, i * U + (u + 3))
                            dve.wait_ge(y_full, i * U + (u + 1))
                            nc.vector.tensor_copy(YB[:, u, 512:1024], PS[:, 7, :]).then_inc(y_dve, 1)

            @block.tensor
            def _(pe):
                def slots(u, v):
                    pe.wait_ge(oh_ok, v)
                    for c in range(TL):
                        last = nc.tensor.matmul(PS[:, 5, 0:2], OH[:, c], RHS[:, u, c, 1:3], start=c == 0, stop=c == TL - 1)
                    last.then_inc(idx_full, 1)

                def transpose_x(u, arrived):
                    pe.wait_ge(x_ld[u], arrived)
                    for k in range(KD):
                        last = nc.tensor.transpose(PS[:, 2 + k // 4, (k % 4) * P:(k % 4 + 1) * P], XB[:, u, k * P:(k + 1) * P], ident)
                    last.then_inc(xT_full, 1)

                slots(0, 1)
                slots(1, 2)
                transpose_x(0, 16)
                n_rounds = rounds(pe)
                with pe.Fori(0, ITERS) as i:
                    with pe.If(i < n_rounds):
                        for u in range(U):
                            pe.wait_ge(xT_out, i * U + (u + 1))
                            for m, (bank, w) in enumerate(((0, EG[u]), (1, EU[u]))):
                                pe.wait_ge(w_ld[m][u], i * 16 + 16)
                                for k in range(KD):
                                    last = nc.tensor.matmul(PS[:, bank, 0:FF], XBT[:, u, k, :], w[:, k, :], start=k == 0, stop=k == KD - 1)
                                last.then_inc(used[m][u], 1)
                            transpose_x((u + 1) % U, i * 16 + (32 if u == U - 1 else 16))
                            pe.wait_ge(hid2_ok, i * U + (u + 1))
                            for c in range(2):
                                last = nc.tensor.transpose(PS[:, 4, c * P:(c + 1) * P], HB[:, u, c * P:(c + 1) * P], ident)
                            last.then_inc(h2T_full, 1)
                            pe.wait_ge(idx_ok, i * U + (u + 2))
                            slots((u + 2) % U, i * U + (u + 3))
                            pe.wait_ge(h2T_out, i * U + (u + 1))
                            pe.wait_ge(w_ld[2][u], i * 16 + 16)
                            for half in range(2):
                                for c in range(2):
                                    last = nc.tensor.matmul(PS[:, 6 + half, :], HBT[:, u, c, :], ED[u][:, c, half * 512:(half + 1) * 512],
                                                            start=c == 0, stop=c == 1)
                            last.then_inc(y_full, 1)
        if upto == 4:
            return

        YL = ring(0, TL * D).rearrange("p (t n) -> p t n", t=TL)
        TB2 = pr(0, 2 * D).rearrange("p (b n) -> p b n", b=2)
        RF = pr(2 * D, 2 * TL).rearrange("p (t n) -> p t n", n=2)
        yl_ld = [sem(f"yl_ld{i}") for i in range(TL)]
        fin_sq, fin_sd, fin_ok, out_st = (sem(n) for n in ("fin_sq", "fin_sd", "fin_ok", "out_st"))
        with nc.Block() as block:
            @block.sync
            def _(sp):
                for i in range(TL):
                    sp.dma_start(YL[:, i], y_dram[i * P:(i + 1) * P, :]).then_inc(yl_ld[i], 16)
                for i in range(TL):
                    sp.wait_ge(fin_ok, i + 1)
                    sp.dma_start(out[0, i * P:(i + 1) * P, :], X[:, i]).then_inc(out_st, 16)
                sp.wait_ge(out_st, 16 * TL)

            @block.scalar
            def _(act):
                for i in range(TL):
                    act.wait_ge(yl_ld[i], 16)
                    if i >= 2:
                        act.wait_ge(fin_ok, i - 1)
                    nc.scalar.activation(TB2[:, i % 2], YL[:, i], ACT.Square, accum_out=RF[:, i, 0:1]).then_inc(fin_sq, 1)
                    act.wait_ge(fin_sq, i + 1)
                    nc.scalar.activation(RF[:, i, 1:2], RF[:, i, 0:1], ACT.Sqrt, bias=const("eps"), scale=1.0 / D).then_inc(fin_sd, 1)

            @block.vector
            def _(dve):
                for i in range(TL):
                    dve.wait_ge(fin_sd, i + 1)
                    own(dve, dve_own, dve_n, nc.vector.reciprocal(RF[:, i, 1:2], RF[:, i, 1:2]))
                    own(dve, dve_own, dve_n, nc.vector.scalar_tensor_tensor(out=TB2[:, i % 2], in0=YL[:, i], scalar=RF[:, i, 1:2], in1=BC[:, 3],
                                                                            op0=ALU.mult, op1=ALU.mult))
                    nc.vector.tensor_tensor(X[:, i], X[:, i], TB2[:, i % 2], ALU.add).then_inc(fin_ok, 1)


NAMES = ["x", "c", "ctx", "c_ctx", "w_mod", "b_mod", "norm_g", "w_in", "ret_log_decay", "ret_norm_g", "mlstm_conv_w",
         "mlstm_conv_b", "mlstm_gate_b", "mlstm_norm_g", "w_out", "w_router", "router_bias", "w_gate", "w_up", "w_down",
         "ws_gate", "ws_up", "ws_down"]


def kernel(**inputs):
    import numpy as _np
    import concourse.bacc as _bacc
    from concourse import mybir as _mybir
    from concourse.bass_utils import run_bass_kernel_spmd as _run

    nc = _bacc.Bacc("TRN2", target_bir_lowering=False, num_devices=1)
    arrays, args = {}, {}
    for name in NAMES + ["consts"]:
        a = constants() if name == "consts" else _np.ascontiguousarray(inputs[name])
        arrays[f"in_{name}"] = a
        args[name] = nc.dram_tensor(f"in_{name}", a.shape, _mybir.dt.from_np(a.dtype), kind="ExternalInput").ap()
    out = nc.dram_tensor("out_0", (1, SEQ, D), F32, kind="ExternalOutput").ap()
    build(nc, args, out)
    r = _run(nc, [arrays], core_ids=[0])
    return r.results[0]["out_0"]
```

```python
from contextlib import ExitStack

import numpy as np

import concourse.bass as bass
from concourse import mybir

F32 = mybir.dt.float32
I32 = mybir.dt.int32
U32 = mybir.dt.uint32
ALU = mybir.AluOpType
ACT = mybir.ActivationFunctionType
AX = mybir.AxisListType

P = 128
D = 1024
KD = D // P
SEQ, CTX = 512, 256
TL, TC = SEQ // P, CTX // P
H = 4
HD = 128
W = H * HD
CHUNKS = TL + TC
GRID_W = 64
NE, TOPK, NG = 64, 8, 8
FF = 256
ROUTED_SCALE = 2.5
EPS = 1e-6
SCALE = HD ** -0.5
BIG = 1e30
U = 3
MAX_BLOCKS = NE + SEQ * TOPK // P - 1
ITERS = -(-MAX_BLOCKS // U)
LIST = U * ITERS + 4
CODES = NE + 1
LEVELS = SEQ // P
SMALL = P // 2
KINDS_FULL = 3 * U
TRASH = SEQ

CONST = {}
_at = 0
for _name, _n in [("ident", P), ("iota", P), ("iota64", P), ("ones", P), ("le", P), ("lt", P), ("relp", P), ("reln", P),
                  ("negf", P), ("negb", P), ("ge", P), ("p", 1), ("rp", 1), ("p1", 1), ("rp1", 1),
                  ("trash", 1), ("half", 1), ("slot", 1), ("tok1", TL), ("eps", 1), ("sel", H * P), ("cos", TL * 64), ("sin", TL * 64)]:
    CONST[_name] = (_at, _at + _n)
    _at += _n
NCONST = _at


def constants():
    c = np.zeros((P, NCONST), np.float32)
    p = np.arange(P, dtype=np.float32)[:, None]
    m = np.arange(P, dtype=np.float32)[None, :]

    def put(name, v):
        a, b = CONST[name]
        c[:, a:b] = v
    put("ident", np.eye(P))
    put("iota", np.broadcast_to(m, (P, P)))
    put("iota64", np.broadcast_to(m % 64, (P, P)))
    put("ones", 1.0)
    put("le", p <= m)
    put("lt", p < m)
    put("ge", p >= m)
    put("relp", np.maximum(m - p, 0))
    put("reln", np.maximum(p - m, 0))
    put("negf", np.where(m >= p, 0.0, BIG))
    put("negb", np.where(m <= p, 0.0, BIG))
    put("p", p)
    put("rp", P - 1 - p)
    put("p1", p + 1)
    put("rp1", P - p)
    put("trash", TRASH + 1 + p)
    put("half", (p >= 64) - 2.0)
    put("slot", p % U * 3)
    put("tok1", p + 1 + P * np.arange(TL)[None, :])
    put("eps", EPS)
    sel = np.zeros((P, H, P), np.float32)
    for h in range(H):
        sel[h, h] = 1.0
    put("sel", sel.reshape(P, -1))
    quarter = HD // 4
    freqs = np.float32(10000.0) ** (-np.arange(quarter, dtype=np.float32) / np.float32(quarter))
    tok = np.arange(SEQ)
    ang = np.concatenate([(tok // GRID_W).astype(np.float32)[:, None] * freqs,
                          (tok % GRID_W).astype(np.float32)[:, None] * freqs], -1).astype(np.float32)
    lay = lambda a: a.reshape(TL, P, 64).transpose(1, 0, 2).reshape(P, -1)
    put("cos", lay(np.cos(ang)))
    put("sin", lay(np.sin(ang)))
    return c


def project_jobs():
    jobs = [("vec", None, 0)]
    jobs += [("mod1", s, s) for s in range(4)]
    jobs += [("modT", None, 0)]
    for k in range(KD):
        jobs += [("xT", None, k), ("xcT", None, k)]
    jobs += [("mk", 4, h) for h in range(H)] + [("mkc", 4, h) for h in range(H)]
    jobs += [("gate", None, 0)]
    jobs += [("mod2", 5, 0)]
    jobs += [("mv", 6, t) for t in range(TL + TC)]
    jobs += [("mkT", None, t) for t in range(TL + TC)]
    jobs += [("mod2", 7, 1)]
    jobs += [("rk", 8, t) for t in range(TL + TC)]
    jobs += [("mod2", 9, 2)]
    jobs += [("rv", 10, t) for t in range(TL + TC)]
    jobs += [("rkT", None, t) for t in range(TL)]
    jobs += [("mod2", 11, 3)]
    jobs += [("mq", 12, h) for h in range(H)]
    jobs += [("mod2", 13, 4)]
    jobs += [("rq", 14, t) for t in range(2)]
    jobs += [("rqT", None, 0), ("rq", 14, 2), ("rqT", None, 1), ("rq", 14, 3)]
    jobs += [("mod2", 15, 5)]
    jobs += [("rg", 16, t) for t in range(TL)]
    jobs += [("rqT", None, 2), ("rqT", None, 3)]
    jobs += [("mod2", 17, 6)]
    jobs += [("mo", 18, t) for t in range(TL)]
    jobs += [("mod2", 19, 7)]
    return jobs


IN_SLABS = {4: 5 * W, 6: 6 * W, 8: W, 10: 2 * W, 12: 4 * W, 14: 0, 16: 3 * W, 18: 7 * W}
SLABS = 20
NSLOT = 3
NBANK = 6
MOD_TILES = 4


def build(nc, t, out, upto=5):
    ctx = ExitStack()
    with ctx:
        def sb(name, shape, dt=F32):
            return ctx.enter_context(nc.sbuf_tensor(name, shape, dt))

        def sem(name):
            return ctx.enter_context(nc.semaphore(name))

        h_dram = nc.dram_tensor("h_rows", (SEQ, D), F32, kind="Internal").ap()
        y_dram = nc.dram_tensor("y_rows", (SEQ + P, D), F32, kind="Internal").ap()
        m_dram = nc.dram_tensor("mod_rows", (4, D), F32, kind="Internal").ap()

        CT = sb("CT", [P, NCONST])
        X = sb("X", [P, TL, D])
        RING = sb("RING", [P, U * 6144])
        PR = sb("PR", [P, 24600])
        ST = sb("ST", [P, 2056])
        DM = sb("DM", [P, H, P])
        VECT = sb("VECT", [P, 72])
        MODS = sb("MODS", [P, P])
        CC = sb("CC", [P, 2 * (KD - 1) + 32])
        MM = sb("MM", [P, 2, 16])
        MODA = sb("MODA", [P, 2, KD])
        SS = sb("SS", [P, 6])
        RST = sb("RST", [P, 6])
        WG = sb("WG", [P, KD, 16])
        GT = sb("GT", [P, CHUNKS, 16])
        COL = sb("COL", [P, 12, 16])
        LG = sb("LG", [P, 8])
        RARG = sb("RARG", [P, 3, 8])
        RDEC = sb("RDEC", [P, 3, 8])
        DPB = sb("DPB", [P, H, 12])
        GB = sb("GB", [4, 4])
        MST = sb("MST", [4, 2, 8])
        DEN = sb("DEN", [P, 8])
        IDX = sb("IDX", [P, U, 3], U32)
        WCOL = sb("WCOL", [P, U, 1])
        TOK = sb("TOK", [P, U, 1])
        RHS = sb("RHS", [P, U, TL, 3])

        PS = ctx.enter_context(nc.psum_tensor("PS", [P, 8, 512], F32))

        def const(name, rows=P):
            a, b = CONST[name]
            return CT[0:rows, a:b]

        def ring(a, n, rows=P):
            return RING[0:rows, a:a + n]

        def pr(a, n, rows=P):
            return PR[0:rows, a:a + n]

        def heads(ap, m=HD):
            return ap.rearrange("p (t h d) -> p t h d", h=H, d=m)

        ident = const("ident")
        cos = const("cos").rearrange("p (t d) -> p t d", t=TL)
        sin = const("sin").rearrange("p (t d) -> p t d", t=TL)
        sel = const("sel").rearrange("p (h m) -> p h m", h=H)
        BLI = CT[0:1, CONST["sel"][0]:CONST["sel"][0] + 4 * LIST + NE + 2].bitcast(I32)

        slots = [ring(s * 4096, 4096).rearrange("p (k n) -> p k n", k=KD) for s in range(NSLOT)]
        HT = ring(12288, 4096).rearrange("p (k n) -> p k n", k=KD)
        HTC = ring(16384, 2048).rearrange("p (k n) -> p k n", k=KD)

        RK = heads(pr(0, 2048))
        RV = heads(pr(2048, 2048))
        MQT = pr(4096, 2048).rearrange("p (h n) -> p h n", h=H)
        MKT = pr(6144, 2048).rearrange("p (h n) -> p h n", h=H)
        MK = heads(pr(8192, 2048))
        RQT = pr(10240, 2048).rearrange("p (h n) -> p h n", h=H)
        RKT = pr(12288, 2048).rearrange("p (h n) -> p h n", h=H)
        MV = heads(pr(14336, 2064), 129)
        RKC = heads(pr(16400, 1024))
        RVC = heads(pr(17424, 1024))
        MVC = heads(pr(18448, 1032), 129)
        MKC = heads(pr(19480, 1024))
        RG = pr(20504, 2048).rearrange("p (t n) -> p t n", t=TL)
        MO = pr(22552, 2048).rearrange("p (t n) -> p t n", t=TL)
        MKTC = pr(10240, 1024).rearrange("p (h n) -> p h n", h=H)
        XN = pr(12288, 6144).rearrange("p (t n) -> p t n", t=6)
        XC = pr(4096, 2048).rearrange("p (t n) -> p t n", t=TC)
        VEC = MODS[0:72, :]
        MODROW = ST[:, 0:512].rearrange("p (s n) -> p s n", s=4)
        ACC = ST[:, 0:1024].rearrange("p (b n) -> p b n", b=2)
        RQS = ST[:, 1024:2048].rearrange("p (b n) -> p b n", b=2)
        TMP1 = pr(22552, 1024).rearrange("p (b n) -> p b n", b=2)

        jobs = project_jobs()
        at = {(what, i): n for n, (what, _, i) in enumerate(jobs)}
        last_of_slab = {s: n for n, (_, s, _) in enumerate(jobs) if s is not None}

        w_mod_v = t["w_mod"][0].rearrange("(k p) n -> p k n", p=P)
        w_in_v = t["w_in"][0].rearrange("(k p) n -> p k n", p=P)

        ld_const, ld_vec, ld_x, ld_xc, ld_wg = (sem(n) for n in ("ld_const", "ld_vec", "ld_x", "ld_xc", "ld_wg"))
        slab_ld = [sem(f"slab_ld{s}") for s in range(NSLOT + 1)]

        def slab(n):
            if n == NSLOT:
                return HT, slab_ld[NSLOT], 16
            slot = n % NSLOT
            return slots[slot], slab_ld[slot], 16 * (n // NSLOT + (slot > 0 or n == 0))
        ps_full = sem("ps_full")
        ps_free = [sem(f"ps_free{b}") for b in range(NBANK)]
        cc_ok, ss_ok, std_ok, xn_ok, moda_ok, silu_ok, rope_own = (sem(n) for n in (
            "cc_ok", "ss_ok", "std_ok", "xn_ok", "moda_ok", "silu_ok", "rope_own"))
        ld_small, rarg_ok, rdec_ok, em_ok, em_used = (sem(n) for n in (
            "ld_small", "rarg_ok", "rdec_ok", "em_ok", "em_used"))
        ms_st, cc_zero = sem("ms_st"), sem("cc_zero")
        dve_own, act_own, pool_own = (sem(n) for n in ("dve_own", "act_own", "pool_own"))

        def own(eng, s, count, ins):
            count[0] += 1
            ins.then_inc(s, 1)
            eng.wait_ge(s, count[0])

        dve_n, act_n, pool_n = [0], [0], [0]

        def evacuated(eng, n):
            eng.wait_ge(ps_free[n % NBANK], n // NBANK + 1)

        def hT_tile(i, k):
            return HT[:, k, i * P:(i + 1) * P] if i < TL else HTC[:, k, (i - TL) * P:(i - TL + 1) * P]

        def decay_tmp(n):
            return TMP1[:, n % 2, 0:P]

        with nc.Block() as block:
            @block.sync
            def _(sp):
                for name, rows, at_row in (("c", 8, 0), ("c_ctx", 8, 8), ("norm0", 8, 16), ("bmod0", 16, 24),
                                           ("conv_w", 24, 40), ("conv_b", 8, 64)):
                    src = {"c": t["c"][0, :], "c_ctx": t["c_ctx"], "norm0": t["norm_g"][0, 0, :],
                           "bmod0": t["b_mod"][0, 0:2048], "conv_w": t["mlstm_conv_w"][0].rearrange("a n -> (a n)"),
                           "conv_b": t["mlstm_conv_b"][0]}[name]
                    sp.dma_start(VEC[at_row:at_row + rows, :], src.rearrange("(r n) -> r n", n=P)).then_inc(ld_vec, 16)
                sp.dma_start(CT[:, :], t["consts"]).then_inc(ld_const, 16)
                for n in range(SLABS):
                    place, loaded, _ = slab(n)
                    if n > NSLOT:
                        sp.wait_ge(ps_full, last_of_slab[n - NSLOT] + 1)
                    if n in IN_SLABS:
                        src = w_in_v[:, :, IN_SLABS[n]:IN_SLABS[n] + 512]
                    else:
                        m = n if n < 4 else 4 + (n - 5) // 2
                        src = w_mod_v[:, :, m * 512:(m + 1) * 512]
                    sp.dma_start(place, src).then_inc(loaded, 16)

            @block.gpsimd
            def _(pool):
                nc.gpsimd.memset(CC[:, 2 * KD:], 0.0).then_inc(cc_zero, 1)
                pool.wait_ge(ps_full, at["xcT", KD - 1] + 1)
                nc.gpsimd.memset(MV[:, :, :, HD:HD + 1], 1.0)
                nc.gpsimd.memset(MVC[:, :, :, HD:HD + 1], 1.0)

            @block.scalar
            def _(act):
                act.dma_start(X[:, :, :], t["x"][0].rearrange("(t p) n -> p t n", p=P)).then_inc(ld_x, 16)
                act.dma_start(XC, t["ctx"][0].rearrange("(t p) n -> p t n", p=P)).then_inc(ld_xc, 16)
                act.dma_start(LG[:, :], t["ret_log_decay"][0].rearrange("a h -> (a h)").partition_broadcast(P)).then_inc(ld_small, 16)
                act.dma_start(WG[:, :, :], w_in_v[:, :, 8 * W:8 * W + 16]).then_inc(ld_wg, 16)
                act.wait_ge(ld_x, 16)
                for i in range(TL):
                    nc.scalar.activation(XN[:, i, :], X[:, i, :], ACT.Square, accum_out=SS[:, i:i + 1]).then_inc(ss_ok, 1)
                act.wait_ge(ld_xc, 16)
                for i in range(TC):
                    nc.scalar.activation(XN[:, TL + i, :], XC[:, i, :], ACT.Square, accum_out=SS[:, TL + i:TL + i + 1]).then_inc(ss_ok, 1)
                evacuated(act, 0)
                nc.scalar.activation(CC[:, 0:2 * KD].rearrange("p (k s) -> p s k", s=2), VECT[:, 0:16].rearrange("p (s k) -> p s k", s=2),
                                     ACT.Silu).then_inc(cc_ok, 1)
                act.wait_ge(ss_ok, 6)
                act.wait_ge(ld_const, 16)
                nc.scalar.activation(RST[:, :], SS[:, :], ACT.Sqrt, bias=const("eps"), scale=1.0 / D).then_inc(std_ok, 1)
                act.wait_ge(ld_small, 16)
                own(act, act_own, act_n, nc.scalar.activation(RARG[:, 0, :], LG[:, :], ACT.Exp))
                own(act, act_own, act_n, nc.scalar.mul(LG[:, :], RARG[:, 0, :], -1.0))
                act.wait_ge(rarg_ok, 1)
                nc.scalar.activation(RDEC[:, :, :], RARG[:, :, :], ACT.Exp).then_inc(rdec_ok, 1)
                for h in range(H):
                    for d, rel in enumerate(("relp", "reln")):
                        n = 2 * h + d
                        if n >= 2:
                            act.wait_ge(em_used, n - 1)
                        nc.scalar.activation(decay_tmp(n), const(rel), ACT.Exp, scale=LG[:, d * 4 + h:d * 4 + h + 1]).then_inc(em_ok, 1)
                n_silu = 0
                for n, (what, _, i) in enumerate(jobs):
                    bank = n % NBANK
                    full = PS[:, bank, :]
                    if what == "vec":
                        continue
                    if what == "modT":
                        act.wait_ge(moda_ok, 1)
                        continue
                    if what == "rq" or what == "rk" and i < TL:
                        continue
                    if what in ("mk", "mkc", "mq"):
                        evacuated(act, n)
                        dst = {"mk": MKT[:, i, :], "mkc": MKTC[:, i, :], "mq": MQT[:, i, :]}[what]
                        nc.scalar.activation(dst, ACC[:, n_silu % 2, 0:(CTX if what == "mkc" else SEQ)], ACT.Silu).then_inc(silu_ok, 1)
                        n_silu += 1
                        continue
                    act.wait_ge(ps_full, n + 1)
                    if what == "mod1":
                        ins = nc.scalar.copy(MODROW[:, i], full[:, 0:P])
                    elif what == "xT":
                        ins = nc.scalar.activation(HT[:, i, :], full, ACT.Identity, bias=MM[:, 0, i:i + 1], scale=MODA[:, 0, i:i + 1])
                    elif what == "xcT":
                        ins = nc.scalar.activation(HTC[:, i, :], full[:, 0:CTX], ACT.Identity, bias=MM[:, 1, i:i + 1], scale=MODA[:, 1, i:i + 1])
                    elif what == "gate":
                        ins = nc.scalar.copy(GT[:, :, :].rearrange("p c n -> p (c n)"), full[:, 0:96])
                    elif what in ("mv", "rv", "rk"):
                        lat, cx = {"mv": (MV, MVC), "rv": (RV, RVC), "rk": (RK, RKC)}[what]
                        dst = lat[:, i] if i < TL else cx[:, i - TL]
                        ins = nc.scalar.copy(dst[:, :, 0:HD], full.rearrange("p (h d) -> p h d", h=H))
                    elif what == "mkT":
                        dst = MK[:, i] if i < TL else MKC[:, i - TL]
                        ins = nc.scalar.copy(dst, full.rearrange("p (h d) -> p h d", h=H))
                    elif what in ("rkT", "rqT"):
                        dst = (RKT if what == "rkT" else RQT)[:, :, i * P:(i + 1) * P]
                        ins = nc.scalar.copy(dst, full.rearrange("p (h d) -> p h d", h=H))
                    elif what == "rg":
                        ins = nc.scalar.activation(RG[:, i, :], full, ACT.Silu)
                    elif what == "mo":
                        ins = nc.scalar.activation(MO[:, i, :], full, ACT.Sigmoid)
                    elif what == "mod2":
                        if i:
                            act.wait_ge(ms_st, 16 * i)
                        ins = nc.scalar.copy(MODS[:, :], full[:, 0:P])
                    ins.then_inc(ps_free[bank], 1)
                    if what == "mod2":
                        evacuated(act, n)
                        dst = m_dram[i // 2, (i % 2) * 512:(i % 2 + 1) * 512].rearrange("(g n) -> g n", n=P)
                        act.dma_start(dst, MODS[0:P:32, :]).then_inc(ms_st, 16)
                act.wait_ge(ms_st, 16 * 8)

            @block.vector
            def _(dve):
                def o(ins):
                    own(dve, dve_own, dve_n, ins)
                dve.wait_ge(ps_full, 1)
                nc.vector.tensor_copy(VECT[:, :], PS[:, 0, 0:72]).then_inc(ps_free[0], 1)
                evacuated(dve, 0)
                dve.wait_ge(ld_const, 16)
                dve.wait_ge(act_own, 2)
                for a, (f, b) in enumerate((("rp", "p"), ("p1", "rp1"))):
                    nc.vector.tensor_scalar(RARG[:, a, 0:4], LG[:, 0:4], const(f), None, ALU.mult)
                    nc.vector.tensor_scalar(RARG[:, a, 4:8], LG[:, 4:8], const(b), None, ALU.mult)
                nc.vector.tensor_scalar(RARG[:, 2, :], LG[:, :], float(P), None, ALU.mult).then_inc(rarg_ok, 1)
                dve.wait_ge(rdec_ok, 1)
                o(nc.vector.tensor_scalar(RDEC[:, 1, :], RDEC[:, 1, :], SCALE, None, ALU.mult))
                for h in range(H):
                    for d, mask in enumerate(("le", "ge")):
                        n = 2 * h + d
                        dve.wait_ge(em_ok, n + 1)
                        if d == 0:
                            ins = nc.vector.scalar_tensor_tensor(out=DM[:, h, :], in0=decay_tmp(n), scalar=SCALE, in1=const(mask), op0=ALU.mult, op1=ALU.mult)
                        else:
                            o(nc.vector.scalar_tensor_tensor(out=decay_tmp(n), in0=decay_tmp(n), scalar=SCALE, in1=const(mask), op0=ALU.mult, op1=ALU.mult))
                            ins = nc.vector.tensor_tensor(DM[:, h, :], DM[:, h, :], decay_tmp(n), ALU.add)
                        ins.then_inc(em_used, 1)
                        dve.wait_ge(em_used, n + 1)
                dve.wait_ge(std_ok, 1)
                o(nc.vector.reciprocal(RST[:, :], RST[:, :]))
                for i in range(6):
                    src = X[:, i, :] if i < TL else XC[:, i - TL, :]
                    nc.vector.tensor_scalar(XN[:, i, :], src, RST[:, i:i + 1], None, ALU.mult).then_inc(xn_ok, 1)
                n_conv = n_rope = 0
                for n, (what, _, i) in enumerate(jobs):
                    bank = n % NBANK
                    full = PS[:, bank, :]
                    if what == "modT":
                        dve.wait_ge(ps_full, n + 1)
                        mt = full.rearrange("p (c r) -> p r c", r=32)[:, 0:2, :]
                        bmod = VECT[:, 24:40].unsqueeze(1).to_broadcast([P, 2, 16])
                        ng0 = VECT[:, 16:24].unsqueeze(1).to_broadcast([P, 2, KD])
                        nc.vector.tensor_tensor(MM[:, :, :], mt, bmod, ALU.add).then_inc(ps_free[bank], 1)
                        evacuated(dve, n)
                        nc.vector.scalar_tensor_tensor(out=MODA[:, :, :], in0=MM[:, :, 8:16], scalar=1.0, in1=ng0,
                                                       op0=ALU.add, op1=ALU.mult).then_inc(moda_ok, 1)
                    elif what in ("mk", "mkc", "mq"):
                        dve.wait_ge(ps_full, n + 1)
                        N = CTX if what == "mkc" else SEQ
                        f = (0 if what == "mq" else H) + i
                        w = [VECT[:, 40 + 8 * j + f:41 + 8 * j + f] for j in range(3)]
                        acc = ACC[:, n_conv % 2, 0:N]
                        if n_conv >= 2:
                            dve.wait_ge(silu_ok, n_conv - 1)
                        o(nc.vector.tensor_scalar(acc, full[:, 0:N], w[1], VECT[:, 64 + f:65 + f], ALU.mult, ALU.add))
                        o(nc.vector.scalar_tensor_tensor(out=acc[:, 1:N], in0=full[:, 0:N - 1], scalar=w[0], in1=acc[:, 1:N], op0=ALU.mult, op1=ALU.add))
                        nc.vector.scalar_tensor_tensor(out=acc[:, 0:N - 1], in0=full[:, 1:N], scalar=w[2], in1=acc[:, 0:N - 1],
                                                       op0=ALU.mult, op1=ALU.add).then_inc(ps_free[bank], 1)
                        n_conv += 1
                    elif what == "rq" or what == "rk" and i < TL:
                        dve.wait_ge(ps_full, n + 1)
                        ph = full.rearrange("p (h s d) -> p h s d", h=H, s=2)
                        cs, sn = (a[:, i, :].unsqueeze(1).to_broadcast([P, H, 64]) for a in (cos, sin))
                        if what == "rk":
                            dst = RK[:, i]
                        else:
                            if i >= 2:
                                dve.wait_ge(ps_full, at["rqT", i - 2] + 1)
                            dst = RQS[:, i % 2, :].rearrange("p (h d) -> p h d", h=H)
                        a, b = (TMP1[:, j, :].rearrange("p (h s d) -> p h s d", h=H, s=2) for j in range(2))
                        for s in range(2):
                            nc.vector.tensor_tensor(a[:, :, s, :], ph[:, :, s, :], cs, ALU.mult)
                            nc.vector.tensor_tensor(b[:, :, s, :], ph[:, :, 1 - s, :], sn, ALU.mult).then_inc(rope_own, 1)
                        dve.wait_ge(rope_own, 2 * n_rope + 2)
                        nc.vector.tensor_tensor(dst[:, :, 0:64], a[:, :, 0, :], b[:, :, 0, :], ALU.subtract)
                        nc.vector.tensor_tensor(dst[:, :, 64:128], a[:, :, 1, :], b[:, :, 1, :], ALU.add).then_inc(ps_free[bank], 1)
                        n_rope += 1
                        evacuated(dve, n)

            @block.tensor
            def _(pe):
                pe.wait_ge(ld_const, 16)
                pe.wait_ge(ld_vec, 16 * 6)
                for n, (what, s, i) in enumerate(jobs):
                    bank = n % NBANK
                    full = PS[:, bank, :]
                    if n >= NBANK:
                        pe.wait_ge(ps_free[bank], n // NBANK)
                    if s is not None:
                        w, loaded, count = slab(s)
                        pe.wait_ge(loaded, count)
                    if what == "vec":
                        last = nc.tensor.transpose(full[:, 0:72], VEC, const("ident", 72)[:, 0:72])
                    elif what in ("mod1", "mod2"):
                        pe.wait_ge(cc_ok, 1)
                        pe.wait_ge(cc_zero, 1)
                        for k in range(KD):
                            vectors = CC[:, 2 * k:2 * k + 32]
                            for g in range(MOD_TILES):
                                last = nc.tensor.matmul(full[g * 32:(g + 1) * 32, 0:P], vectors, w[:, k, g * P:(g + 1) * P],
                                                        start=k == 0, stop=k == KD - 1)
                    elif what == "modT":
                        for s1 in range(4):
                            evacuated(pe, at["mod1", s1])
                        for s1 in range(4):
                            last = nc.tensor.transpose(full[:, s1 * P:(s1 + 1) * P], MODROW[:, s1], ident)
                    elif what in ("xT", "xcT"):
                        pe.wait_ge(xn_ok, 6)
                        for c in range(TL if what == "xT" else TC):
                            src = XN[:, c if what == "xT" else TL + c, i * P:(i + 1) * P]
                            last = nc.tensor.transpose(full[:, c * P:(c + 1) * P], src, ident)
                    elif what in ("mk", "mkc", "mq"):
                        evacuated(pe, at["xcT", KD - 1])
                        h = HTC if what == "mkc" else HT
                        N = CTX if what == "mkc" else SEQ
                        for k in range(KD):
                            last = nc.tensor.matmul(full[:, 0:N], w[:, k, i * HD:(i + 1) * HD], h[:, k, :], start=k == 0, stop=k == KD - 1)
                    elif what == "gate":
                        pe.wait_ge(ld_wg, 16)
                        for c in range(TL + TC):
                            for k in range(KD):
                                last = nc.tensor.matmul(full[:, c * 16:(c + 1) * 16], hT_tile(c, k), WG[:, k, :], start=k == 0, stop=k == KD - 1)
                    elif what == "mkT":
                        pe.wait_ge(silu_ok, 2 * H)
                        src = MKT[:, :, i * P:(i + 1) * P] if i < TL else MKTC[:, :, (i - TL) * P:(i - TL + 1) * P]
                        for h in range(H):
                            last = nc.tensor.transpose(full[:, h * HD:(h + 1) * HD], src[:, h, :], ident)
                    elif what in ("rkT", "rqT"):
                        evacuated(pe, at[what[:2], i])
                        src = RK[:, i] if what == "rkT" else RQS[:, i % 2, :].rearrange("p (h d) -> p h d", h=H)
                        for h in range(H):
                            last = nc.tensor.transpose(full[:, h * HD:(h + 1) * HD], src[:, h, :], ident)
                    else:
                        for k in range(KD):
                            last = nc.tensor.matmul(full, hT_tile(i, k), w[:, k, :], start=k == 0, stop=k == KD - 1)
                    last.then_inc(ps_full, 1)
        if upto == 1:
            return

        UNITS = 2 * CHUNKS
        STEPS = CHUNKS

        def chunk_of(n):
            s, d = divmod(n, 2)
            if s < TC:
                return False, (s if d == 0 else TC - 1 - s)
            return True, (s - TC if d == 0 else TL - 1 - (s - TC))

        def pos_of(n):
            lat, c = chunk_of(n)
            return TC + c if lat else c

        KINDS = {
            "all": list(range(UNITS)),
            "lat": [n for n in range(UNITS) if n // 2 >= TC],
            "intra": [n for n in range(UNITS) if TC <= n // 2 < TC + TL // 2],
            "state": [n for n in range(UNITS) if n // 2 < STEPS - 1],
        }

        def upto_unit(kind, n):
            return sum(u <= n for u in KINDS[kind])

        def wait(eng, s, v):
            if v > 0:
                eng.wait_ge(s, v)

        def rows4(a, n):
            return ring(a, n, 4)

        GR = rows4(0, 3072).rearrange("p (k n) -> p k n", k=4)
        BB = rows4(3072, 1536).rearrange("p (d n) -> p d n", d=2)
        AR = rows4(4608, 1536).rearrange("p (d n) -> p d n", d=2)
        AA = rows4(6144, 1536).rearrange("p (d n) -> p d n", d=2)
        TT = ring(7680, 1536)
        LF = rows4(9216, 1536).rearrange("p (d n) -> p d n", d=2)
        ZF = rows4(10752, 1536).rearrange("p (d n) -> p d n", d=2)
        W1, W2 = LF, ZF
        W3 = rows4(0, 1536).rearrange("p (d n) -> p d n", d=2)
        TTd = TT.rearrange("p (d n) -> p d n", d=2)
        DPE = sb("DPE", [4, 12])
        WO = ring(0, 8192).rearrange("p (k n) -> p k n", k=KD)
        w_out_v = t["w_out"][0].rearrange("(k p) n -> p k n", p=P)
        GAIN = pr(19456, 1024)
        OR = ring(12288, 2048).rearrange("p (t h n) -> p t h n", t=TL, h=H)
        OM = ring(14336, 2048).rearrange("p (t h n) -> p t h n", t=TL, h=H)
        PT = ring(16384, 512).rearrange("p (h n) -> p h n", h=H)
        KDB = ring(16896, 512).rearrange("p (h n) -> p h n", h=H)
        ZE = ring(17408, 512).rearrange("p (h n) -> p h n", h=H)
        PT2 = ring(17920, 512).rearrange("p (h n) -> p h n", h=H)
        KWB = ring(9216, 512).rearrange("p (h n) -> p h n", h=H)
        TI = ring(9728, 516).rearrange("p (a n) -> p a n", a=2)
        ND = ring(10752, 516)
        SR = ST[:, 0:1024].rearrange("p (d h n) -> p d h n", d=2, h=H)
        SM = ST[:, 1024:2056].rearrange("p (d h n) -> p d h n", d=2, h=H)
        ND4 = ND.rearrange("p (h n) -> p h n", h=H)
        TI4 = ring(9728, 516).rearrange("p (h n) -> p h n", h=H)

        ld_gb, gT_full, gT_out, rows_ok, nl_ok, exp_ok, tt_ok, tt_zero = (sem(n) for n in (
            "ld_gb", "gT_full", "gT_out", "rows_ok", "nl_ok", "exp_ok", "tt_ok", "tt_zero"))
        ld_wo, ld_gain, gated = sem("ld_wo"), sem("ld_gain"), sem("gated")
        col_full, col_ok, dpb_full, dpb_ok = (sem(n) for n in ("col_full", "col_ok", "dpb_full", "dpb_ok"))
        r_sc, r_out, r_in, r_st, m_qk, m_a, m_num, m_in, m_st = (sem("pe_" + n) for n in (
            "r_sc", "r_out", "r_in", "r_st", "m_qk", "m_a", "m_num", "m_in", "m_st"))
        pt_ok, or_ok, s_ok, z_ok, pt2_ok, nd_ok, c_ok, om_ok = (sem("dve_" + n) for n in (
            "pt", "or", "s", "z", "pt2", "nd", "c", "om"))
        ro_ok, kd_ok, e_ok, kw_ok, ti_ok = (sem("act_" + n) for n in ("ro", "kd", "e", "kw", "ti"))

        with nc.Block() as block:
            @block.sync
            def _(sp):
                with nc.allow_non_contiguous_dma(reason="sixteen gate biases"):
                    sp.dma_start(GB[:, :], t["mlstm_gate_b"][0].rearrange("g h -> h g")).then_inc(ld_gb, 16)
                sp.wait_ge(col_ok, 3)
                sp.wait_ge(exp_ok, 5)
                sp.dma_start(WO[:, 0:6], w_out_v[:, 0:6]).then_inc(ld_wo, 16)
                sp.wait_ge(kw_ok, 2 * TC)
                sp.wait_ge(m_st, 2 * TC)
                sp.dma_start(GAIN[:, 0:W], t["ret_norm_g"][0].partition_broadcast(P)).then_inc(ld_gain, 16)
                sp.dma_start(GAIN[:, W:2 * W], t["mlstm_norm_g"][0].partition_broadcast(P)).then_inc(ld_gain, 16)

            @block.gpsimd
            def _(pool):
                nc.gpsimd.memset(TT, 0.0).then_inc(tt_zero, 1)
                pool.wait_ge(ld_gain, 32)
                for i in range(TL):
                    nc.gpsimd.tensor_tensor(RG[:, i], RG[:, i], GAIN[:, 0:W], ALU.mult)
                    nc.gpsimd.tensor_tensor(MO[:, i], MO[:, i], GAIN[:, W:2 * W], ALU.mult).then_inc(gated, 1)

            @block.scalar
            def _(act):
                for g in range(CHUNKS):
                    pos = TC + g if g < TL else g - TL
                    act.wait_ge(gT_full, g + 1)
                    nc.scalar.copy(GR[:, :, pos * P:(pos + 1) * P],
                                   PS[0:4, g, :].rearrange("p (k n) -> p k n", k=4)).then_inc(gT_out, 1)
                act.wait_ge(rows_ok, 1)
                own(act, act_own, act_n, nc.scalar.activation(LF, LF, ACT.Exp))
                nc.scalar.activation(LF, LF, ACT.Ln, bias=const("ones", 4)[:, 0:1]).then_inc(nl_ok, 1)
                act.wait_ge(tt_zero, 1)
                act.wait_ge(rows_ok, 2)
                nc.scalar.copy(TTd[0:4], AR).then_inc(exp_ok, 1)
                nc.scalar.activation(TTd[32:36], W1, ACT.Exp).then_inc(exp_ok, 1)
                nc.scalar.activation(TTd[64:68], W2, ACT.Exp, scale=-1.0).then_inc(exp_ok, 1)
                nc.scalar.activation(TTd[96:100], W3, ACT.Exp, scale=-1.0).then_inc(exp_ok, 1)
                nc.scalar.activation(DPE[:, :], DPE[:, :], ACT.Exp).then_inc(exp_ok, 1)
                act.wait_ge(col_ok, 3)
                for n in range(UNITS):
                    lat, c = chunk_of(n)
                    d = n % 2
                    k_ret, k_ml = (RK[:, c], MK[:, c]) if lat else (RKC[:, c], MKC[:, c])
                    if n in KINDS["state"]:
                        wait(act, r_st, upto_unit("state", n - 1))
                        for h in range(H):
                            ins = nc.scalar.activation(KDB[:, h], k_ret[:, h], ACT.Copy, scale=RDEC[:, 0, 4 * d + h:4 * d + h + 1])
                        ins.then_inc(kd_ok, 1)
                        wait(act, m_st, upto_unit("state", n - 1))
                        for h in range(H):
                            ins = nc.scalar.activation(KWB[:, h], k_ml[:, h], ACT.Copy, scale=COL[:, n, 4 + h:5 + h])
                        ins.then_inc(kw_ok, 1)
                    if not lat:
                        continue
                    act.wait_ge(z_ok, upto_unit("lat", n))
                    nc.scalar.activation(ZE, ZE, ACT.Exp, scale=-1.0).then_inc(e_ok, 1)
                    if n in KINDS["intra"]:
                        act.wait_ge(r_out, upto_unit("intra", n))
                        nc.scalar.copy(OR[:, c], PS[:, 1, :].rearrange("p (h n) -> p h n", h=H)).then_inc(ro_ok, 1)
                    act.wait_ge(m_in, upto_unit("lat", n))
                    wait(act, nd_ok, upto_unit("lat", n - 1))
                    for h in range(H):
                        ins = nc.scalar.activation(TI4[:, h], PS[:, h // 2, (h % 2) * 129:(h % 2) * 129 + 129], ACT.Copy,
                                                   scale=COL[:, n, 8 + h:9 + h])
                    ins.then_inc(ti_ok, 1)

            @block.vector
            def _(dve):
                def o(ins):
                    own(dve, dve_own, dve_n, ins)
                o(nc.vector.memset(MST[:, :, 0:1], 0.0))
                dve.wait_ge(gT_out, CHUNKS)
                dve.wait_ge(ld_gb, 16)
                for d in range(2):
                    o(nc.vector.tensor_scalar(ZF[:, d], GR[:, 2 * d + 1], GB[:, 2 * d + 1:2 * d + 2], None, ALU.add))
                nc.vector.scalar_tensor_tensor(out=LF, in0=ZF, scalar=-1.0, in1=ZF, op0=ALU.mult, op1=ALU.min).then_inc(rows_ok, 1)
                dve.wait_ge(nl_ok, 1)
                o(nc.vector.scalar_tensor_tensor(out=LF, in0=ZF, scalar=0.0, in1=LF, op0=ALU.min, op1=ALU.subtract))

                def row(a, d, pos):
                    lo, hi = pos * P, (pos + 1) * P
                    return a[:, d, lo:hi] if d == 0 else a[:, d, lo:hi][:, ::-1]

                for n in range(UNITS):
                    last = nc.vector.tensor_tensor_scan(row(BB, n % 2, pos_of(n)), const("ones", 4), row(LF, n % 2, pos_of(n)), 0.0,
                                                        op0=ALU.mult, op1=ALU.add)
                o(last)
                for d in range(2):
                    o(nc.vector.scalar_tensor_tensor(out=AR[:, d], in0=GR[:, 2 * d], scalar=GB[:, 2 * d:2 * d + 1], in1=BB[:, d],
                                                     op0=ALU.add, op1=ALU.subtract))
                for s in range(STEPS):
                    for d in range(2):
                        n = 2 * s + d
                        a = row(AR, d, pos_of(n))
                        ins = nc.vector.tensor_tensor_scan(row(AA, d, pos_of(n)), a, a, MST[:, d, s:s + 1], op0=ALU.max, op1=ALU.max)
                    o(ins)
                    for d in range(2):
                        n = 2 * s + d
                        end = pos_of(n) * P + (P - 1 if d == 0 else 0)
                        nc.vector.tensor_tensor(MST[:, d, s + 1:s + 2], BB[:, d, end:end + 1], AA[:, d, end:end + 1], ALU.add)
                        ins = nc.vector.tensor_tensor(DPE[:, n:n + 1], MST[:, d, s:s + 1], AA[:, d, end:end + 1], ALU.subtract)
                    o(ins)
                for n in range(UNITS):
                    s, d = divmod(n, 2)
                    lo = pos_of(n) * P
                    end = lo + (P - 1 if d == 0 else 0)
                    nc.vector.tensor_scalar(W1[:, d, lo:lo + P], AR[:, d, lo:lo + P], AA[:, d, end:end + 1], None, ALU.subtract)
                    nc.vector.tensor_scalar(W2[:, d, lo:lo + P], AA[:, d, lo:lo + P], MST[:, d, s:s + 1], None, ALU.subtract)
                nc.vector.tensor_tensor(W3, BB, AA, ALU.add).then_inc(rows_ok, 1)
                for b in range(3):
                    dve.wait_ge(col_full, b + 1)
                    src = PS[:, b, :].rearrange("p (n q m) -> p n q m", n=4, q=4)[:, :, :, 0:4]
                    dst = COL[:, 4 * b:4 * b + 4, :].rearrange("p n (q m) -> p n q m", q=4)
                    o(nc.vector.tensor_copy(dst, src))
                    nc.vector.tensor_scalar(COL[:, 4 * b:4 * b + 4, 4:8], COL[:, 4 * b:4 * b + 4, 4:8], SCALE, None, ALU.mult).then_inc(col_ok, 1)
                dve.wait_ge(col_ok, 3)
                dve.wait_ge(dpb_full, 1)
                nc.vector.tensor_copy(DPB[:, :, :], PS[:, 3, 0:48].rearrange("p (h n) -> p h n", h=H)).then_inc(dpb_ok, 1)
                dve.wait_ge(dpb_ok, 1)
                for n in range(UNITS):
                    lat, c = chunk_of(n)
                    s, d = divmod(n, 2)
                    neg = const("negf" if d == 0 else "negb")
                    if lat:
                        if n in KINDS["intra"]:
                            dve.wait_ge(r_sc, upto_unit("intra", n))
                            wait(dve, r_out, upto_unit("intra", n - 1))
                            nc.vector.tensor_tensor(PT, PS[:, 0, :].rearrange("p (h n) -> p h n", h=H), DM[:, :, :], ALU.mult).then_inc(pt_ok, 1)
                        dve.wait_ge(m_a, upto_unit("lat", n))
                        wait(dve, pt2_ok, upto_unit("lat", n - 1))
                        for h in range(H):
                            ins = nc.vector.scalar_tensor_tensor(out=ZE[:, h], in0=PS[:, 5, h * P:(h + 1) * P], scalar=COL[:, n, h:h + 1],
                                                                 in1=neg, op0=ALU.subtract, op1=ALU.max)
                        ins.then_inc(z_ok, 1)
                        dve.wait_ge(r_in, upto_unit("lat", n))
                        if n in KINDS["intra"]:
                            dve.wait_ge(ro_ok, upto_unit("intra", n))
                        for h in range(H):
                            ins = nc.vector.scalar_tensor_tensor(out=OR[:, c, h], in0=PS[:, 2, h * P:(h + 1) * P],
                                                                 scalar=RDEC[:, 1, 4 * d + h:4 * d + h + 1], in1=OR[:, c, h],
                                                                 op0=ALU.mult, op1=ALU.add)
                        ins.then_inc(or_ok, 1)
                    if n in KINDS["state"]:
                        dve.wait_ge(r_st, upto_unit("state", n))
                        kv = PS[:, 3, :].rearrange("p (h n) -> p h n", h=H)
                        if lat:
                            dve.wait_ge(r_in, upto_unit("lat", n))
                        if s == 0:
                            ins = nc.vector.tensor_copy(SR[:, d], kv)
                        else:
                            for h in range(H):
                                ins = nc.vector.scalar_tensor_tensor(out=SR[:, d, h], in0=SR[:, d, h], scalar=RDEC[:, 2, 4 * d + h:4 * d + h + 1],
                                                                     in1=kv[:, h], op0=ALU.mult, op1=ALU.add)
                        ins.then_inc(s_ok, 1)
                        wait(dve, s_ok, upto_unit("state", n))
                    if lat:
                        dve.wait_ge(e_ok, upto_unit("lat", n))
                        dve.wait_ge(m_qk, upto_unit("lat", n))
                        wait(dve, m_num, upto_unit("lat", n - 1))
                        nc.vector.scalar_tensor_tensor(out=PT2, in0=PS[:, 4, :].rearrange("p (h n) -> p h n", h=H), scalar=SCALE, in1=ZE,
                                                       op0=ALU.mult, op1=ALU.mult).then_inc(pt2_ok, 1)
                        dve.wait_ge(m_num, upto_unit("lat", n))
                        dve.wait_ge(ti_ok, upto_unit("lat", n))
                        nc.vector.tensor_tensor(ND.rearrange("p (a n) -> p a n", a=2), PS[:, 6:8, 0:258], TI, ALU.add).then_inc(nd_ok, 1)
                        dve.wait_ge(nd_ok, upto_unit("lat", n))
                        o(nc.vector.scalar_tensor_tensor(out=DEN[:, 0:4], in0=ND4[:, :, HD], scalar=-1.0, in1=ND4[:, :, HD],
                                                         op0=ALU.mult, op1=ALU.max))
                        o(nc.vector.tensor_tensor(DEN[:, 0:4], DEN[:, 0:4], COL[:, n, 12:16], ALU.max))
                        o(nc.vector.reciprocal(DEN[:, 4:8], DEN[:, 0:4]))
                        for h in range(H):
                            if n in KINDS["intra"]:
                                ins = nc.vector.tensor_scalar(OM[:, c, h], ND4[:, h, 0:HD], DEN[:, 4 + h:5 + h], None, ALU.mult)
                            else:
                                ins = nc.vector.scalar_tensor_tensor(out=OM[:, c, h], in0=ND4[:, h, 0:HD], scalar=DEN[:, 4 + h:5 + h],
                                                                     in1=OM[:, c, h], op0=ALU.mult, op1=ALU.add)
                        ins.then_inc(om_ok, 1)
                        dve.wait_ge(om_ok, upto_unit("lat", n))
                    if n in KINDS["state"]:
                        dve.wait_ge(m_st, upto_unit("state", n))
                        if lat:
                            dve.wait_ge(m_in, upto_unit("lat", n))
                        kv = PS[:, 4:6, 0:258].rearrange("p a (h n) -> p a h n", h=2)
                        if s == 0:
                            ins = nc.vector.tensor_copy(SM[:, d].rearrange("p (a h) n -> p a h n", a=2), kv)
                        else:
                            for h in range(H):
                                ins = nc.vector.scalar_tensor_tensor(out=SM[:, d, h], in0=SM[:, d, h], scalar=DPB[:, h, n:n + 1],
                                                                     in1=kv[:, h // 2, h % 2], op0=ALU.mult, op1=ALU.add)
                        ins.then_inc(c_ok, 1)
                        dve.wait_ge(c_ok, upto_unit("state", n))

            @block.tensor
            def _(pe):
                for g in range(CHUNKS):
                    for k in range(4):
                        last = nc.tensor.transpose(PS[0:4, g, k * P:(k + 1) * P], GT[:, g, 4 * k:4 * k + 4], ident)
                    last.then_inc(gT_full, 1)
                pe.wait_ge(exp_ok, 5)
                for n in range(UNITS):
                    lo = (n % 2) * (CHUNKS * P) + pos_of(n) * P
                    last = nc.tensor.transpose(PS[:, n // 4, (n % 4) * P:(n % 4 + 1) * P], TT[:, lo:lo + P], ident)
                    if n % 4 == 3:
                        last.then_inc(col_full, 1)
                for h in range(H):
                    last = nc.tensor.matmul(PS[:, 3, h * 12:(h + 1) * 12], sel[0:4, h, :], DPE[:, :], start=True, stop=True)
                last.then_inc(dpb_full, 1)
                pe.wait_ge(dpb_ok, 1)
                for n in range(UNITS):
                    lat, c = chunk_of(n)
                    s, d = divmod(n, 2)
                    cs = slice(c * P, (c + 1) * P)
                    v_ret, v_ml = (RV[:, c], MV[:, c]) if lat else (RVC[:, c], MVC[:, c])
                    if lat:
                        if n in KINDS["intra"]:
                            wait(pe, ti_ok, upto_unit("lat", n - 1))
                            for h in range(H):
                                last = nc.tensor.matmul(PS[:, 0, h * P:(h + 1) * P], RKT[:, h, cs], RQT[:, h, cs], start=True, stop=True)
                            last.then_inc(r_sc, 1)
                        wait(pe, c_ok, upto_unit("state", n - 1))
                        wait(pe, pt2_ok, upto_unit("lat", n - 1))
                        lo = pos_of(n) * P
                        for h in range(H):
                            last = nc.tensor.matmul(PS[:, 5, h * P:(h + 1) * P], sel[0:4, h, :], AA[:, d, lo:lo + P], start=True, stop=True)
                        last.then_inc(m_a, 1)
                        for h in range(H):
                            last = nc.tensor.matmul(PS[:, 4, h * P:(h + 1) * P], MKT[:, h, cs], MQT[:, h, cs], start=True, stop=True)
                        last.then_inc(m_qk, 1)
                        wait(pe, or_ok, upto_unit("lat", n - 1))
                        wait(pe, s_ok, upto_unit("state", n - 2))
                        for h in range(H):
                            last = nc.tensor.matmul(PS[:, 2, h * P:(h + 1) * P], RQT[:, h, cs], SR[:, d, h], start=True, stop=True)
                        last.then_inc(r_in, 1)
                        if n in KINDS["intra"]:
                            pe.wait_ge(pt_ok, upto_unit("intra", n))
                            for h in range(H):
                                last = nc.tensor.matmul(PS[:, 1, h * P:(h + 1) * P], PT[:, h], v_ret[:, h], start=True, stop=True)
                            last.then_inc(r_out, 1)
                    if n in KINDS["state"]:
                        pe.wait_ge(kd_ok, upto_unit("state", n))
                        wait(pe, s_ok, upto_unit("state", n - 1))
                        for h in range(H):
                            last = nc.tensor.matmul(PS[:, 3, h * P:(h + 1) * P], KDB[:, h], v_ret[:, h], start=True, stop=True)
                        last.then_inc(r_st, 1)
                    if lat:
                        wait(pe, c_ok, upto_unit("state", n - 2))
                        if n in KINDS["intra"]:
                            pe.wait_ge(ro_ok, upto_unit("intra", n))
                        wait(pe, ti_ok, upto_unit("lat", n - 1))
                        for h in range(H):
                            last = nc.tensor.matmul(PS[:, h // 2, (h % 2) * 129:(h % 2) * 129 + 129], MQT[:, h, cs], SM[:, d, h], start=True, stop=True)
                        last.then_inc(m_in, 1)
                        pe.wait_ge(pt2_ok, upto_unit("lat", n))
                        wait(pe, nd_ok, upto_unit("lat", n - 1))
                        for h in range(H):
                            last = nc.tensor.matmul(PS[:, 6 + h // 2, (h % 2) * 129:(h % 2) * 129 + 129], PT2[:, h], v_ml[:, h], start=True, stop=True)
                        last.then_inc(m_num, 1)
                    if n in KINDS["state"]:
                        pe.wait_ge(kw_ok, upto_unit("state", n))
                        wait(pe, c_ok, upto_unit("state", n - 1))
                        for h in range(H):
                            last = nc.tensor.matmul(PS[:, 4 + h // 2, (h % 2) * 129:(h % 2) * 129 + 129], KWB[:, h], v_ml[:, h], start=True, stop=True)
                        last.then_inc(m_st, 1)
        if upto == 2:
            return

        WR = ring(8192, 512).rearrange("p (k n) -> p k n", k=KD)
        RB = ring(8704, NE)
        SHG = pr(0, 2048).rearrange("p (k n) -> p k n", k=KD)
        SHU = pr(2048, 2048).rearrange("p (k n) -> p k n", k=KD)
        SHD = pr(4096, 2048).rearrange("p (c n) -> p c n", c=2)
        HT2 = pr(6144, 4096).rearrange("p (k n) -> p k n", k=KD)
        BC = pr(10240, 4096).rearrange("p (m n) -> p m n", m=4)
        YN = pr(14336, 1024)
        YT = [pr(15360, 1024).rearrange("p (k n) -> p k n", k=KD),
              CT[:, CONST["sel"][0]:CONST["sel"][0] + 1024].rearrange("p (k n) -> p k n", k=KD)]
        TB = pr(16384, 1024)
        HP = pr(17408, 2048).rearrange("p (b n) -> p b n", b=2)
        FOLD = [ring(8768, 1024), ring(9792, 1024), ring(10816, 1024), ring(16384, 1024), ring(17408, 1024), ST[:, 0:1024], ST[:, 1024:2048]]
        SHS = ST[:, 0:512].rearrange("p (b n) -> p b n", b=2)
        SHH = ST[:, 512:1024].rearrange("p (b n) -> p b n", b=2)
        SHT = ST[:, 1024:1536].rearrange("p (b c n) -> p b c n", b=2, c=2)
        SHY = pr(14336, 2048).rearrange("p (b n) -> p b n", b=2)
        ZERO = pr(16384, 1024)
        RWL = pr(22520, 2080).rearrange("p (t l c w) -> p t l c w", t=TL, l=LEVELS, w=2)
        RWLc = pr(22520, 2080).rearrange("p (t c w) -> p t c w", t=TL, w=2)
        BNS = ring(11840, 48).rearrange("p (j n) -> p j n", n=6)
        MVR = ring(11888, 16).rearrange("p (j n) -> p j n", n=2)
        R2 = ring(11904, 4 * TL).rearrange("p (t n) -> p t n", n=4)
        def rt(a, n):
            return pr(20504 + a, n)
        SC = rt(0, 256).rearrange("p (t e) -> p t e", t=TL)
        SEL = rt(256, 64)
        SELM = rt(320, 64)
        REP = rt(384, 64)
        MSK = rt(448, 256).rearrange("p (t e) -> p t e", t=TL)
        WGT = rt(704, 256).rearrange("p (t e) -> p t e", t=TL)
        M8 = rt(960, 64)
        GRP = rt(1024, 12)
        G8 = rt(1036, 12)
        GRR = rt(1048, 12)
        GMK = rt(1060, 8)
        GNEG = rt(1068, 8)
        T8 = rt(1076, 8)
        WS = rt(1084, 2)
        CNT = rt(1090, 4)
        PEND = rt(1096, 1)
        CMP = rt(1100, LIST)
        CMP2 = rt(1200, LIST)
        NTOK = rt(1300, 1)
        JST = rt(1302, 4 * LIST + 2 + NE)
        BLF = pr(19456, 6 * LIST, 1).rearrange("p (a n) -> p a n", a=6)

        ld_wr, ld_sh, ld_bc, ld_fold, ld_rb = (sem("ld_" + n) for n in ("wr", "sh", "bc", "fold", "rb"))
        bn_ok, sd_ok, yn_ok, yT_full, yT_out, z_full, z_out, sq_ok, x1_ok, sq2_ok, hp_ok, h_st, h_st2, hT_full, hT_out = (sem("c_" + n) for n in (
            "bn", "sd", "yn", "yTf", "yTo", "zf", "zo", "sq", "x1", "sq2", "hp", "hst", "hst2", "hTf", "hTo"))
        r_out, sc_in, r_full, sc_ok, sg_full, su_full, ss_silu, hid_ok, sT_full, sT_out, sd_full, sd_out, y_st, zero_ok = (sem("c_" + n) for n in (
            "ro", "scin", "rf", "sc", "sgf", "suf", "silu", "hid", "sTf", "sTo", "sdf", "sdo", "yst", "zero"))
        y_st2 = sem("c_yst2")
        sc_done = sem("sc_done")
        msk_ok, rank_full, cnt_full, cmp_in, cmp_ok, list_full, pend_full, bl_ok = (sem("c_" + n) for n in (
            "msk", "rankf", "cntf", "cmpin", "cmp", "listf", "pendf", "bl"))
        h_st_s, y_st_s = [h_st, h_st2], [y_st, y_st2]

        weights = [("w_gate", 0, "e (p k) n -> e p (k n)", KD), ("w_up", 2048, "e (p k) n -> e p (k n)", KD),
                   ("w_down", 4096, "e (k p) n -> e p k n", 2)]
        w_src = [t[name][0].rearrange(how, k=k) for name, _, how, k in weights]

        w_ld = [[sem(f"{name}_ld{u}") for u in range(U)] for name, *_ in weights]

        def load(eng, m, e, u):
            dst, src = ring(u * 6144 + weights[m][1], 2048), w_src[m][bass.ds(e, 1)]
            if m < 2:
                src = src.rearrange("e p n -> (e p) n")
            else:
                dst, src = dst.rearrange("p (k n) -> p k n", k=2), src.rearrange("e p k n -> (e p) k n")
            eng.dma_start(dst, src).then_inc(w_ld[m][u], 16)

        def z_banks(i):
            return PS[:, 2 + 2 * (i % 2):4 + 2 * (i % 2), :]

        def router_tile(dve, o, i):
            sc3 = SEL.rearrange("p (g e) -> p g e", g=NG)
            o(nc.vector.tensor_tensor(SEL, SC[:, i], RB, ALU.add))
            for g in range(NG):
                last = nc.vector.max(M8[:, g * 8:(g + 1) * 8], SEL[:, g * 8:(g + 1) * 8])
            o(last)
            m8 = M8.rearrange("p (g e) -> p g e", g=NG)
            o(nc.vector.tensor_tensor(GRP[:, 0:8], m8[:, :, 0], m8[:, :, 1], ALU.add))
            o(nc.vector.max(G8[:, 0:8], GRP[:, 0:8]))
            o(nc.vector.memset(G8[:, 4:8], -BIG))
            o(nc.vector.match_replace(out=GRR, in_to_replace=G8[:, 0:8], in_values=GRP, imm_value=-2 * BIG))
            o(nc.vector.tensor_tensor(GMK, GRR[:, 0:8], GRP[:, 0:8], ALU.not_equal))
            o(nc.vector.tensor_scalar(GNEG, GMK, 1.0, BIG, ALU.subtract, ALU.mult))
            gm = GMK.unsqueeze(2).to_broadcast([P, NG, 8])
            gn = GNEG.unsqueeze(2).to_broadcast([P, NG, 8])
            sm = SELM.rearrange("p (g e) -> p g e", g=NG)
            o(nc.vector.tensor_tensor(sm, sc3, gm, ALU.mult))
            o(nc.vector.tensor_tensor(sm, sm, gn, ALU.add))
            o(nc.vector.max(T8, SELM))
            o(nc.vector.match_replace(out=REP, in_to_replace=T8, in_values=SELM, imm_value=-2 * BIG))
            nc.vector.tensor_tensor(MSK[:, i], REP, SELM, ALU.not_equal).then_inc(msk_ok, 1)
            dve.wait_ge(msk_ok, i + 1)
            o(nc.vector.tensor_tensor(WGT[:, i], SC[:, i], MSK[:, i], ALU.mult))
            o(nc.vector.reduce_sum(WS[:, 0:1], WGT[:, i], AX.X))
            o(nc.vector.reciprocal(WS[:, 1:2], WS[:, 0:1]))
            o(nc.vector.tensor_scalar(WGT[:, i], WGT[:, i], WS[:, 1:2], ROUTED_SCALE, ALU.mult, ALU.mult))

        with nc.Block() as block:
            @block.sync
            def _(sp):
                sp.dma_start(WO[:, 6:KD], w_out_v[:, 6:KD]).then_inc(ld_wo, 16)
                for m in range(4):
                    sp.dma_start(BC[:, m], m_dram[m].partition_broadcast(P)).then_inc(ld_bc, 16)
                for dst, src in zip(FOLD, [t["b_mod"][0, (2 + m) * D:(3 + m) * D] for m in range(4)] + [t["norm_g"][0, m] for m in (1, 2, 3)]):
                    sp.dma_start(dst, src.partition_broadcast(P)).then_inc(ld_fold, 16)
                sp.dma_start(WR, t["w_router"][0].rearrange("(p k) n -> p k n", k=KD)).then_inc(ld_wr, 16)
                sp.dma_start(RB, t["router_bias"][0].partition_broadcast(P)).then_inc(ld_rb, 16)
                sp.dma_start(SHG, t["ws_gate"][0].rearrange("(p k) n -> p k n", k=KD)).then_inc(ld_sh, 16)
                sp.dma_start(SHU, t["ws_up"][0].rearrange("(p k) n -> p k n", k=KD)).then_inc(ld_sh, 16)
                sp.dma_start(SHD, t["ws_down"][0].rearrange("(p c) n -> p c n", c=2)).then_inc(ld_sh, 16)
                for i in range(TL):
                    sp.wait_ge(hp_ok, i + 1)
                    sp.dma_start(h_dram[i * P:(i + 1) * P, :], HP[:, i % 2]).then_inc(h_st_s[i % 2], 16)
                sp.wait_ge(z_full, TL)
                for m in range(3):
                    load(sp, m, 0, 0)
                load(sp, 0, 1, 1)
                sp.wait_ge(hp_ok, TL)
                load(sp, 2, 1, 1)
                for m in range(2):
                    load(sp, m, 2, 2)
                sp.wait_ge(r_full, TL)
                sp.wait_ge(msk_ok, TL)
                load(sp, 1, 1, 1)
                for s in h_st_s + y_st_s:
                    sp.wait_ge(s, 16 * TL // 2)

            @block.gpsimd
            def _(pool):
                pool.wait_ge(zero_ok, 1)
                for lo in (0, SMALL):
                    pool.dma_start(y_dram[TRASH + lo:TRASH + lo + SMALL, :], ZERO[lo:lo + SMALL]).then_inc(sc_done, 16)
                pool.wait_ge(su_full, TL)
                nc.gpsimd.memset(pr(0, 1024 * U), 0.0)
                pool.wait_ge(sc_done, 32)

            @block.scalar
            def _(act):
                def norm_std(i, dst, src_ss):
                    return nc.scalar.activation(dst, src_ss, ACT.Sqrt, bias=const("eps"), scale=1.0 / D)

                def mixed(i):
                    act.wait_ge(bn_ok, i + 1)
                    nc.scalar.activation(MVR[:, :, 1], MVR[:, :, 1], ACT.Sqrt, bias=const("eps")).then_inc(sd_ok, 1)
                    act.wait_ge(yT_full, i + 1)
                    if i >= 2:
                        act.wait_ge(z_full, i - 1)
                    nc.scalar.copy(YT[i % 2].rearrange("p (b k) n -> p b (k n)", b=2), PS[:, 0:2, :]).then_inc(yT_out, 1)

                def residual(i):
                    act.wait_ge(z_full, i + 1)
                    nc.scalar.activation(TB.rearrange("p (b n) -> p b n", b=2), z_banks(i), ACT.Square, accum_out=R2[:, i, 0:1]).then_inc(sq_ok, 1)
                    act.wait_ge(sq_ok, i + 1)
                    norm_std(i, R2[:, i, 1:2], R2[:, i, 0:1]).then_inc(z_out, 1)
                    act.wait_ge(x1_ok, i + 1)
                    own(act, act_own, act_n, nc.scalar.activation(TB, X[:, i], ACT.Square, accum_out=R2[:, i, 2:3]))
                    norm_std(i, R2[:, i, 3:4], R2[:, i, 2:3]).then_inc(sq2_ok, 1)
                    act.wait_ge(hT_full, i + 1)
                    nc.scalar.copy(HT2[:, :, i * P:(i + 1) * P], PS[:, 6:8, :].rearrange("p b (k n) -> p (b k) n", n=P)).then_inc(hT_out, 1)
                    act.wait_ge(r_full, i + 1)
                    nc.scalar.copy(SC[:, i], z_banks(i)[:, 0, 0:NE]).then_inc(r_out, 1)

                mixed(0)
                mixed(1)
                mixed(2)
                residual(0)
                mixed(3)
                for i in range(1, TL):
                    residual(i)
                act.wait_ge(r_out, TL)
                nc.scalar.activation(SC, SC, ACT.Sigmoid).then_inc(sc_ok, 1)
                for i in range(TL):
                    act.wait_ge(sg_full, i + 1)
                    if i >= 2:
                        act.wait_ge(hid_ok, i - 1)
                    nc.scalar.activation(SHS[:, i % 2], PS[:, 0, 0:FF], ACT.Silu).then_inc(ss_silu, 1)
                    act.wait_ge(sT_full, i + 1)
                    nc.scalar.copy(SHT[:, i % 2], PS[:, 4, 0:FF].rearrange("p (c n) -> p c n", c=2)).then_inc(sT_out, 1)
                    act.wait_ge(sd_full, i + 1)
                    if i >= 2:
                        act.wait_ge(y_st_s[i % 2], 16 * (i // 2))
                    nc.scalar.copy(SHY[:, i % 2, 0:512], PS[:, 2, :]).then_inc(sd_out, 1)
                    nc.scalar.copy(SHY[:, i % 2, 512:1024], PS[:, 3, :]).then_inc(sd_out, 1)
                    act.wait_ge(sd_out, 2 * i + 2)
                    act.dma_start(y_dram[i * P:(i + 1) * P, :], SHY[:, i % 2]).then_inc(y_st_s[i % 2], 16)

            @block.vector
            def _(dve):
                def o(ins):
                    own(dve, dve_own, dve_n, ins)

                def head_norms(i):
                    if i:
                        dve.wait_ge(yT_full, i)
                    for m, src in enumerate((OR, OM)):
                        for h in range(H):
                            last = nc.vector.bn_stats(BNS[:, m * H + h, :], src[:, i, h])
                    o(last)
                    for j in range(8):
                        last = nc.vector.bn_aggr(MVR[:, j, :], BNS[:, j, :])
                    last.then_inc(bn_ok, 1)
                    dve.wait_ge(sd_ok, i + 1)
                    o(nc.vector.reciprocal(MVR[:, :, 1], MVR[:, :, 1]))
                    for m, src in enumerate((OR, OM)):
                        for h in range(H):
                            j = m * H + h
                            last = nc.vector.tensor_scalar(YN[:, j * HD:(j + 1) * HD], src[:, i, h], MVR[:, j, 0:1], MVR[:, j, 1:2],
                                                           ALU.subtract, ALU.mult)
                    o(last)
                    dve.wait_ge(gated, i + 1)
                    nc.vector.tensor_tensor(YN[:, 0:W], YN[:, 0:W], RG[:, i], ALU.mult)
                    nc.vector.tensor_tensor(YN[:, W:2 * W], YN[:, W:2 * W], MO[:, i], ALU.mult).then_inc(yn_ok, 1)

                def residual(i):
                    dve.wait_ge(z_out, i + 1)
                    o(nc.vector.reciprocal(R2[:, i, 1:2], R2[:, i, 1:2]))
                    o(nc.vector.scalar_tensor_tensor(out=TB.rearrange("p (b n) -> p b n", b=2), in0=z_banks(i), scalar=R2[:, i, 1:2],
                                                     in1=BC[:, 0].rearrange("p (b n) -> p b n", b=2), op0=ALU.mult, op1=ALU.mult))
                    nc.vector.tensor_tensor(X[:, i], X[:, i], TB, ALU.add).then_inc(x1_ok, 1)
                    dve.wait_ge(sq2_ok, i + 1)
                    o(nc.vector.reciprocal(R2[:, i, 3:4], R2[:, i, 3:4]))
                    o(nc.vector.scalar_tensor_tensor(out=TB, in0=X[:, i], scalar=R2[:, i, 3:4], in1=BC[:, 2], op0=ALU.mult, op1=ALU.mult))
                    if i >= 2:
                        dve.wait_ge(h_st_s[i % 2], 16 * (i // 2))
                        dve.wait_ge(hT_full, i - 1)
                    nc.vector.tensor_tensor(HP[:, i % 2].rearrange("q (k p) -> q p k", k=KD), TB.rearrange("q (p k) -> q p k", k=KD),
                                            BC[:, 1].rearrange("q (p k) -> q p k", k=KD), ALU.add).then_inc(hp_ok, 1)
                    dve.wait_ge(hp_ok, i + 1)

                head_norms(0)
                head_norms(1)
                dve.wait_ge(ld_bc, 64)
                dve.wait_ge(ld_fold, 16 * 7)
                for m in range(4):
                    last = nc.vector.tensor_tensor(BC[:, m], BC[:, m], FOLD[m], ALU.add)
                o(last)
                nc.vector.tensor_tensor(BC[:, 0], BC[:, 0], FOLD[4], ALU.mult)
                nc.vector.scalar_tensor_tensor(out=BC[:, 2], in0=BC[:, 2], scalar=1.0, in1=FOLD[5], op0=ALU.add, op1=ALU.mult)
                o(nc.vector.tensor_tensor(BC[:, 3], BC[:, 3], FOLD[6], ALU.mult))
                head_norms(2)
                residual(0)
                head_norms(3)
                residual(1)
                residual(2)
                residual(3)
                dve.wait_ge(yT_full, TL)
                nc.vector.memset(ZERO, 0.0).then_inc(zero_ok, 1)
                nc.vector.memset(GRP[:, 8:12], -BIG)
                o(nc.vector.memset(RWL, -1.0))
                dve.wait_ge(sc_ok, 1)
                dve.wait_ge(ld_rb, 16)

                def hidden(i):
                    dve.wait_ge(su_full, i + 1)
                    dve.wait_ge(ss_silu, i + 1)
                    if i >= 2:
                        dve.wait_ge(sT_full, i - 1)
                    nc.vector.tensor_tensor(SHH[:, i % 2].rearrange("p (c n) -> p n c", c=2), SHS[:, i % 2].rearrange("p (n c) -> p n c", c=2),
                                            PS[:, 1, 0:FF].rearrange("p (n c) -> p n c", c=2), ALU.mult).then_inc(hid_ok, 1)

                hidden(0)
                router_tile(dve, o, 0)
                router_tile(dve, o, 1)
                hidden(1)
                router_tile(dve, o, 2)
                router_tile(dve, o, 3)
                dve.wait_ge(rank_full, 1)
                rank = PS[:, 6, 256:512].rearrange("p (t e) -> p t e", t=TL)
                rk1 = SC
                o(nc.vector.scalar_tensor_tensor(out=rk1, in0=rank, scalar=1.0, in1=MSK, op0=ALU.add, op1=ALU.mult))
                for l in range(LEVELS):
                    nc.vector.tensor_scalar(RWL[:, :, l, 0:NE, 0], rk1, 1.0 + l * P, None, ALU.subtract)
                    last = nc.vector.tensor_copy(RWL[:, :, l, 0:NE, 1], WGT)
                o(last)
                dve.wait_ge(cnt_full, 1)
                cnt = PS[0:NE, 7, 0:1]
                nc.vector.tensor_copy(NTOK[0:NE], cnt)
                o(nc.vector.tensor_scalar(CNT[0:NE, 0:1], cnt, 0.0, None, ALU.is_gt))
                for l in range(1, LEVELS):
                    nc.vector.scalar_tensor_tensor(out=CNT[0:NE, 0:1], in0=cnt, scalar=float(l * P), in1=CNT[0:NE, 0:1],
                                                   op0=ALU.is_gt, op1=ALU.add).then_inc(cmp_in, 1)
                    dve.wait_ge(cmp_in, l)
                hidden(2)
                dve.wait_ge(pend_full, 1)
                o(nc.vector.tensor_copy(PEND[0:NE], PS[0:NE, 7, 1:2]))
                o(nc.vector.tensor_scalar(CMP[0:NE, :], const("iota", NE)[:, 0:LIST], PEND[0:NE], None, ALU.is_ge))
                o(nc.vector.tensor_tensor(PEND[0:NE], PEND[0:NE], CNT[0:NE, 0:1], ALU.subtract))
                nc.vector.scalar_tensor_tensor(out=CMP2[0:NE, :], in0=const("iota", NE)[:, 0:LIST], scalar=PEND[0:NE], in1=CMP[0:NE, :],
                                               op0=ALU.is_ge, op1=ALU.subtract).then_inc(cmp_ok, 1)
                hidden(3)
                dve.wait_ge(list_full, 1)
                o(nc.vector.tensor_copy(JST[0:1, :], PS[0:1, 7, 2:4 + 4 * LIST + NE]))
                e_j, st_j, n_j, slot_j = (JST[0:1, m * LIST:(m + 1) * LIST] for m in range(4))
                total = JST[0:1, 4 * LIST:4 * LIST + 1]
                code, expert, small, kind, level, full = (BLF[:, m, :] for m in range(6))
                o(nc.vector.tensor_tensor(level, const("iota", 1)[:, 0:LIST], st_j, ALU.subtract))
                o(nc.vector.tensor_scalar(level, level, float(LEVELS - 1), None, ALU.min))
                nc.vector.scalar_tensor_tensor(out=code, in0=level, scalar=float(CODES), in1=e_j, op0=ALU.mult, op1=ALU.add)
                nc.vector.tensor_scalar(expert, e_j, float(NE - 1), None, ALU.min)
                o(nc.vector.scalar_tensor_tensor(out=full, in0=level, scalar=float(-P), in1=n_j, op0=ALU.mult, op1=ALU.add))
                o(nc.vector.tensor_scalar(small, full, float(SMALL), None, ALU.is_le))
                o(nc.vector.scalar_tensor_tensor(out=kind, in0=small, scalar=float(KINDS_FULL), in1=slot_j, op0=ALU.mult, op1=ALU.add))
                o(nc.vector.tensor_copy(BLI[:, 0:4 * LIST], BLF[:, 0:4, :].rearrange("p a n -> p (a n)")))
                nc.vector.tensor_scalar(BLI[:, 4 * LIST:4 * LIST + NE + 1], JST[0:1, 4 * LIST + 1:], 1.0, None, ALU.add)
                o(nc.vector.tensor_scalar(full[:, 0:ITERS], const("iota", 1)[:, 0:ITERS], float(U), total, ALU.mult, ALU.is_lt))
                o(nc.vector.reduce_sum(full[:, ITERS:ITERS + 1], full[:, 0:ITERS], AX.X))
                nc.vector.tensor_copy(BLI[:, 4 * LIST + NE + 1:], full[:, ITERS:ITERS + 1]).then_inc(bl_ok, 1)
                dve.wait_ge(bl_ok, 1)
                for u in range(U):
                    nc.vector.tensor_copy(RHS[:, u, :, 2], const("tok1"))

            @block.tensor
            def _(pe):
                def transpose_y(i):
                    pe.wait_ge(yn_ok, i + 1)
                    if i:
                        pe.wait_ge(yT_out, i)
                    for k in range(KD):
                        last = nc.tensor.transpose(PS[:, k // 4, (k % 4) * P:(k % 4 + 1) * P], YN[:, k * P:(k + 1) * P], ident)
                    last.then_inc(yT_full, 1)

                def project_y(i, half):
                    if half == 0:
                        pe.wait_ge(yT_out, i + 1)
                        pe.wait_ge(ld_wo, 32)
                        if i >= 2:
                            pe.wait_ge(x1_ok, i - 1)
                            pe.wait_ge(r_out, i - 1)
                    for k in range(KD):
                        last = nc.tensor.matmul(z_banks(i)[:, half, :], YT[i % 2][:, k, :], WO[:, k, half * 512:(half + 1) * 512],
                                                start=k == 0, stop=k == KD - 1)
                    if half:
                        last.then_inc(z_full, 1)

                def transpose_h(i):
                    pe.wait_ge(hp_ok, i + 1)
                    if i:
                        pe.wait_ge(hT_out, i)
                    for k in range(KD):
                        last = nc.tensor.transpose(PS[:, 6 + k // 4, (k % 4) * P:(k % 4 + 1) * P], HP[:, i % 2, k * P:(k + 1) * P], ident)
                    last.then_inc(hT_full, 1)

                def router(i):
                    pe.wait_ge(hT_out, i + 1)
                    pe.wait_ge(ld_wr, 16)
                    for k in range(KD):
                        last = nc.tensor.matmul(z_banks(i)[:, 0, 0:NE], HT2[:, k, i * P:(i + 1) * P], WR[:, k, :], start=k == 0, stop=k == KD - 1)
                    last.then_inc(r_full, 1)

                def shared(i):
                    pe.wait_ge(hT_out, i + 1)
                    pe.wait_ge(ld_sh, 48)
                    if i == 0:
                        pe.wait_ge(yT_out, TL)
                    else:
                        pe.wait_ge(hid_ok, i)
                    for bank, w, done in ((0, SHG, sg_full), (1, SHU, su_full)):
                        for k in range(KD):
                            last = nc.tensor.matmul(PS[:, bank, 0:FF], HT2[:, k, i * P:(i + 1) * P], w[:, k, :], start=k == 0, stop=k == KD - 1)
                        last.then_inc(done, 1)

                def shared_down(i):
                    pe.wait_ge(hid_ok, i + 1)
                    if i == 0:
                        pe.wait_ge(r_out, TL)
                    else:
                        pe.wait_ge(sT_out, i)
                        pe.wait_ge(sd_out, 2 * i)
                    for c in range(2):
                        last = nc.tensor.transpose(PS[:, 4, c * P:(c + 1) * P], SHH[:, i % 2, c * P:(c + 1) * P], ident)
                    last.then_inc(sT_full, 1)
                    pe.wait_ge(sT_out, i + 1)
                    for half in range(2):
                        for c in range(2):
                            last = nc.tensor.matmul(PS[:, 2 + half, :], SHT[:, i % 2, c, :], SHD[:, c, half * 512:(half + 1) * 512], start=c == 0, stop=c == 1)
                    last.then_inc(sd_full, 1)

                transpose_y(0)
                for i in range(TL):
                    project_y(i, 0)
                    if i < TL - 1:
                        transpose_y(i + 1)
                    project_y(i, 1)
                    if i:
                        transpose_h(i - 1)
                        router(i - 1)
                shared(0)
                transpose_h(TL - 1)
                router(TL - 1)
                shared_down(0)
                shared(1)
                shared_down(1)
                pe.wait_ge(msk_ok, TL)
                for i in range(TL):
                    out_i = PS[:, 6, 256 + i * NE:256 + (i + 1) * NE]
                    for j in range(i + 1):
                        last = nc.tensor.matmul(out_i, const("lt" if j == i else "ones"), MSK[:, j], start=j == 0, stop=j == i)
                last.then_inc(rank_full, 1)
                for i in range(TL):
                    last = nc.tensor.matmul(PS[0:NE, 7, 0:1], MSK[:, i], const("ones")[:, 0:1], start=i == 0, stop=i == TL - 1)
                last.then_inc(cnt_full, 1)
                shared(2)
                pe.wait_ge(cmp_in, LEVELS - 1)
                nc.tensor.matmul(PS[0:NE, 7, 1:2], const("le", NE)[:, 0:NE], CNT[0:NE, 0:1], start=True, stop=True).then_inc(pend_full, 1)
                shared_down(2)
                shared(3)
                pe.wait_ge(cmp_ok, 1)
                nc.tensor.matmul(PS[0:1, 7, 2:2 + LIST], const("ones", NE)[:, 0:1], CMP[0:NE, :], start=True, stop=True)
                nc.tensor.matmul(PS[0:1, 7, 2 + LIST:2 + 2 * LIST], CNT[0:NE, 0:1], CMP[0:NE, :], start=True, stop=True)
                nc.tensor.matmul(PS[0:1, 7, 2 + 2 * LIST:2 + 3 * LIST], NTOK[0:NE, 0:1], CMP2[0:NE, :], start=True, stop=True)
                nc.tensor.matmul(PS[0:1, 7, 2 + 3 * LIST:2 + 4 * LIST], const("slot", NE), CMP2[0:NE, :], start=True, stop=True)
                nc.tensor.matmul(PS[0:1, 7, 2 + 4 * LIST:3 + 4 * LIST], CNT[0:NE, 0:1], const("ones", NE)[:, 0:1], start=True, stop=True)
                nc.tensor.matmul(PS[0:1, 7, 3 + 4 * LIST:4 + 4 * LIST + NE], CNT[0:NE, 0:1], const("lt", NE)[:, 0:NE + 1], start=True, stop=True).then_inc(list_full, 1)
                shared_down(3)
        if upto == 3:
            return

        XB = pr(0, 1024 * U).rearrange("p (u n) -> p u n", u=U)
        XBT = pr(3072, 1024 * U).rearrange("p (u k n) -> p u k n", u=U, k=KD)
        YB = pr(6144, 1024 * U).rearrange("p (u n) -> p u n", u=U)
        OH = pr(9216, 512).rearrange("p (t n) -> p t n", t=TL)
        SG = pr(14336, FF * U).rearrange("p (u n) -> p u n", u=U)
        HB = pr(15104, FF * U).rearrange("p (u n) -> p u n", u=U)
        HBT = pr(15872, FF * U).rearrange("p (u n) -> p u n", u=U)
        EQ = pr(16640, U)
        EQ2 = pr(16644, U)
        WSLOT = RING.rearrange("p (s n) -> p s n", n=2048)
        y_half = y_dram.rearrange("r (s n) -> (r s) n", s=2)
        CODE, EXPERT, SMALLS, KIND, BEFORE1 = (m * LIST for m in range(5))

        def entry(eng, what, j, hi):
            return eng.value_load(BLI[0:1, bass.ds(j + what, 1)], min_val=0, max_val=hi)

        x_ld = [sem(f"x_ld{u}") for u in range(U)]
        gu_full = sem("e_guf")
        gu_arrived, down_arrived = sem("gu_arrived"), sem("down_arrived")
        rhs_ok, oh_ok, idx_full, eq_ok, idx_ok, xT_full, xT_out = (sem("e_" + n) for n in (
            "rhs", "oh", "idxf", "eq", "idx", "xTf", "xTo"))
        silu2_ok, hid2_ok, h2T_full, h2T_out, y_full, y_act, y_dve = (sem("e_" + n) for n in (
            "silu", "hid", "hTf", "hTo", "yf", "yact", "ydve"))

        sidx_ok, cleared = sem("e_sidx"), sem("cleared")
        gather_go, scatter_go = sem("gather_go"), sem("scatter_go")

        def rounds(eng):
            return eng.snap(eng.value_load(BLI[0:1, 4 * LIST + NE + 1:4 * LIST + NE + 2], min_val=1, max_val=ITERS))

        with nc.Block() as block:
            @block.sync
            def _(sp):
                def gu_complete(u, count):
                    for m in range(2):
                        sp.wait_ge(w_ld[m][u], count)
                    sp.sem_inc(gu_arrived, 1)

                def down_complete(u, count):
                    sp.wait_ge(w_ld[2][u], count)
                    sp.sem_inc(down_arrived, 1)

                def blocks_before(e):
                    return sp.snap(sp.value_load(BLI[0:1, bass.ds(e + BEFORE1, 1)], min_val=1, max_val=MAX_BLOCKS + 1))

                def step(e, u, count):
                    gu_done, down_done = blocks_before(e - 2), blocks_before(e - 3)
                    sp.wait_ge(gu_full, gu_done)
                    for m in range(2):
                        load(sp, m, e, u)
                    sp.wait_ge(y_full, down_done)
                    load(sp, 2, e - 1, (u - 1) % U)
                    gu_complete((u - 1) % U, count)
                    down_complete((u - 2) % U, count if u != 1 else count + (-16))

                for u in range(U - 1):
                    gu_complete(u, 16)
                down_complete(0, 16)
                with sp.Fori(1, NE // U) as i:
                    for u in range(U):
                        step(i * U + u, u, i * 16 + (16 if u else 0))
                step(NE - 1, 0, 16 * ((NE - 2) // U + 1))
                sp.wait_ge(y_full, blocks_before(NE - U))
                load(sp, 2, NE - 1, 0)
                gu_complete(0, 16 * ((NE - 1) // U + 1))
                down_complete(2, 16 * ((NE - 2) // U + 1))
                down_complete(0, 16 * ((NE - 1) // U + 1))

            @block.gpsimd
            def _(pool):
                def gather(j, u, v):
                    small = pool.snap(entry(pool, SMALLS, j, 1))
                    pool.wait_ge(idx_ok, v)
                    pool.sem_inc(gather_go, 1)
                    with pool.If(small > 0):
                        nc.gpsimd.indirect_dma_start(
                            out=XB[0:SMALL, u], out_offset=None, in_=h_dram,
                            in_offset=bass.IndirectOffsetOnAxis(ap=IDX[0:SMALL, u, 0:1], axis=0)).then_inc(x_ld[u], 16)
                    with pool.Else():
                        nc.gpsimd.indirect_dma_start(
                            out=XB[:, u], out_offset=None, in_=h_dram,
                            in_offset=bass.IndirectOffsetOnAxis(ap=IDX[:, u, 0:1], axis=0)).then_inc(x_ld[u], 16)
                for u in range(U):
                    gather(u, u, u + 1)
                pool.wait_ge(xT_full, 1)
                gather(U, 0, U + 1)
                n_rounds = rounds(pool)
                with pool.Fori(0, ITERS) as i:
                    with pool.If(i < n_rounds):
                        for u in range(U):
                            pool.wait_ge(xT_full, i * U + (u + 2))
                            gather(i * U + (u + 4), (u + 1) % U, i * U + (u + 5))
                            small = pool.snap(entry(pool, SMALLS, i * U + u, 1))
                            pool.wait_ge(y_act, i * U + (u + 2))
                            pool.wait_ge(y_dve, i * U + (u + 1))
                            pool.wait_ge(sidx_ok, i * U + (u + 1))
                            pool.wait_ge(sc_done, i * (16 * U) + 16 * (u + 2))
                            pool.sem_inc(scatter_go, 1)
                            with pool.If(small > 0):
                                nc.gpsimd.indirect_dma_start(
                                    out=y_half, out_offset=bass.IndirectOffsetOnAxis(ap=IDX[:, u, 2:3], axis=0),
                                    in_=YB[:, u, 0:512], in_offset=None, compute_op=ALU.add).then_inc(sc_done, 16)
                            with pool.Else():
                                nc.gpsimd.indirect_dma_start(
                                    out=y_dram, out_offset=bass.IndirectOffsetOnAxis(ap=IDX[:, u, 1:2], axis=0),
                                    in_=YB[:, u], in_offset=None, compute_op=ALU.add).then_inc(sc_done, 16)
                        pool.sem_inc(scatter_go, 1)
                pool.wait_ge(sc_done, n_rounds * (16 * U) + 32)
                pool.wait_ge(x_ld[U - 1], n_rounds * 16 + 16)
                pool.wait_ge(x_ld[0], n_rounds * 16 + 32)

            @block.scalar
            def _(act):
                def silu(u, v):
                    act.wait_ge(gu_full, v + 1)
                    nc.scalar.activation(SG[:, u], PS[:, 0, 0:FF], ACT.Silu).then_inc(silu2_ok, 1)

                def xT_evacuate(u, v):
                    act.wait_ge(xT_full, v)
                    for half in range(2):
                        ins = nc.scalar.copy(XBT[:, u, half * 4:half * 4 + 4, :], PS[:, 2 + half, :].rearrange("p (k n) -> p k n", k=4))
                    ins.then_inc(xT_out, 1)

                act.sem_inc(y_act, 1)
                xT_evacuate(0, 1)
                silu(0, 1)
                xT_evacuate(1, 2)
                n_rounds = rounds(act)
                with act.Fori(0, ITERS) as i:
                    with act.If(i < n_rounds):
                        for u in range(U):
                            silu((u + 1) % U, i * U + (u + 2))
                            xT_evacuate((u + 2) % U, i * U + (u + 3))
                            act.wait_ge(sc_done, i * (16 * U) + 16 * (u + 1))
                            act.wait_ge(y_full, i * U + (u + 2))
                            nc.scalar.copy(YB[:, u, 0:512], PS[:, 6, :]).then_inc(y_act, 1)

            @block.vector
            def _(dve):
                def one_hot(j, u, v):
                    code = entry(dve, CODE, j, CODES * LEVELS - 1)
                    nc.vector.tensor_copy(RHS[:, u, :, 0:2], RWLc[:, :, bass.ds(code, 1), :].rearrange("p t c w -> p t (c w)")).then_inc(rhs_ok, 1)
                    small = entry(dve, SMALLS, j, 1)
                    slots = CT[:, bass.ds(small * P + CONST["iota"][0], P)]
                    dve.wait_ge(rhs_ok, v)
                    for c in range(TL):
                        ins = nc.vector.tensor_scalar(OH[:, c], slots, RHS[:, u, c, 0:1], None, ALU.is_equal)
                    ins.then_inc(oh_ok, 1)

                def indices(u, v):
                    dve.wait_ge(idx_full, v)
                    nc.vector.tensor_scalar(IDX[:, u, 0:1], PS[:, 5, 1:2], 1.0, 0.0, ALU.subtract, ALU.max)
                    nc.vector.tensor_copy(WCOL[:, u], PS[:, 5, 0:1])
                    nc.vector.tensor_copy(TOK[:, u], PS[:, 5, 1:2]).then_inc(idx_ok, 1)

                def scatter_index(u, v):
                    dve.wait_ge(idx_ok, v)
                    nc.vector.tensor_scalar(EQ[:, u:u + 1], TOK[:, u], 0.0, const("trash"), ALU.is_equal, ALU.mult).then_inc(eq_ok, 1)
                    dve.wait_ge(eq_ok, v + v + (-1))
                    nc.vector.tensor_scalar(EQ2[:, u:u + 1], EQ[:, u:u + 1], 2.0, const("half"), ALU.mult, ALU.add).then_inc(eq_ok, 1)
                    nc.vector.tensor_scalar(IDX[:, u, 1:2], TOK[:, u], 1.0, EQ[:, u:u + 1], ALU.subtract, ALU.add)
                    dve.wait_ge(eq_ok, v + v)
                    nc.vector.tensor_scalar(IDX[:, u, 2:3], TOK[:, u], 2.0, EQ2[:, u:u + 1], ALU.mult, ALU.add).then_inc(sidx_ok, 1)
                    dve.wait_ge(sidx_ok, v)

                def hidden(u, v):
                    dve.wait_ge(silu2_ok, v)
                    nc.vector.scalar_tensor_tensor(out=HB[:, u], in0=SG[:, u], scalar=WCOL[:, u], in1=PS[:, 0, FF:2 * FF],
                                                   op0=ALU.mult, op1=ALU.mult).then_inc(hid2_ok, 1)

                for u in range(U):
                    one_hot(u, u, u + 1)
                    indices(u, u + 1)
                    if u == 0:
                        for bank in (0, 4, 7):
                            ins = nc.vector.memset(PS[:, bank, :], 0.0)
                        ins.then_inc(cleared, 1)
                hidden(0, 1)
                scatter_index(0, 1)
                one_hot(U, 0, U + 1)
                indices(0, U + 1)
                n_rounds = rounds(dve)
                with dve.Fori(0, ITERS) as i:
                    with dve.If(i < n_rounds):
                        for u in range(U):
                            ahead = (u + 1) % U
                            one_hot(i * U + (u + 4), ahead, i * U + (u + 5))
                            dve.wait_ge(h2T_full, i * U + (u + 1))
                            nc.vector.tensor_copy(HBT[:, u], PS[:, 4, 0:FF]).then_inc(h2T_out, 1)
                            hidden(ahead, i * U + (u + 2))
                            dve.wait_ge(sc_done, i * (16 * U) + 16 * (u + 1))
                            scatter_index(ahead, i * U + (u + 2))
                            dve.wait_ge(y_full, i * U + (u + 2))
                            nc.vector.tensor_copy(YB[:, u, 512:1024], PS[:, 7, :]).then_inc(y_dve, 1)
                            indices(ahead, i * U + (u + 5))

            @block.tensor
            def _(pe):
                def slots(u, v, first=False):
                    if not first:
                        pe.wait_ge(idx_ok, v + (-1))
                    pe.wait_ge(oh_ok, v)
                    for c in range(TL):
                        last = nc.tensor.matmul(PS[:, 5, 0:2], OH[:, c], RHS[:, u, c, 1:3], start=c == 0, stop=c == TL - 1)
                    last.then_inc(idx_full, 1)

                def transpose_x(u, arrived):
                    pe.wait_ge(x_ld[u], arrived)
                    for k in range(KD):
                        last = nc.tensor.transpose(PS[:, 2 + k // 4, (k % 4) * P:(k % 4 + 1) * P], XB[:, u, k * P:(k + 1) * P], ident)
                    last.then_inc(xT_full, 1)

                def gate_up_small(u, s):
                    for k in range(KD):
                        for c in range(2):
                            out_c = PS[c * SMALL:(c + 1) * SMALL, 0, :].rearrange("p (m n) -> p m n", m=2)[:, :, 0:P]
                            last = nc.tensor.matmul(out_c, XBT[:, u, k, 0:SMALL],
                                                    WSLOT[:, 3 * s:3 * s + 2, k * FF + c * P:k * FF + (c + 1) * P], start=k == 0, stop=k == KD - 1)
                    last.then_inc(gu_full, 1)

                def down_small(u, s):
                    for c in range(2):
                        for half in range(2):
                            last = nc.tensor.matmul(PS[half * SMALL:(half + 1) * SMALL, 6, :], HBT[:, u, c * SMALL:(c + 1) * SMALL],
                                                    WSLOT[:, 3 * s + 2, c * 1024 + half * 512:c * 1024 + (half + 1) * 512], start=c == 0, stop=c == 1)
                    last.then_inc(y_full, 1)

                def by_slot(kind, products, u):
                    with pe.If(kind < KINDS_FULL + 3):
                        products(u, 0)
                    with pe.Else():
                        with pe.If(kind < KINDS_FULL + 6):
                            products(u, 1)
                        with pe.Else():
                            products(u, 2)

                def of_block(j):
                    return pe.snap(entry(pe, KIND, j, KINDS_FULL + 3 * (U - 1))), pe.snap(entry(pe, EXPERT, j, NE - 1))

                def gate_up(kind, expert, u, v):
                    pe.wait_ge(gu_arrived, expert + 1)
                    with pe.If(kind > KINDS_FULL - 1):
                        pe.wait_ge(xT_out, v)
                        by_slot(kind, gate_up_small, u)
                    with pe.Else():
                        pe.wait_ge(xT_out, v)
                        slot = nc.s_assert_within(kind, 0, 3 * (U - 1))
                        for k in range(KD):
                            last = nc.tensor.matmul(PS[:, 0, :], XBT[:, u, k, :], WSLOT[:, bass.ds(slot, 2), k * FF:(k + 1) * FF],
                                                    start=k == 0, stop=k == KD - 1)
                        last.then_inc(gu_full, 1)

                n_rounds = rounds(pe)
                pe.sem_inc(gu_full, 1)
                pe.sem_inc(y_full, 1)
                slots(0, 1, first=True)
                slots(1, 2)
                transpose_x(0, 16)
                slots(2, 3)
                pe.wait_ge(cleared, 1)
                this, after = of_block(0), of_block(1)
                gate_up(*this, 0, 1)
                transpose_x(1, 16)
                slots(0, U + 1)
                carried = [pe.alloc_register(name) for name in ("kind0", "expert0", "kind1", "expert1")]

                def carry():
                    for reg, val in zip(carried, (*this, *after)):
                        pe.reg_mov(reg, val)
                carry()
                with pe.Fori(0, ITERS) as i:
                    with pe.If(i < n_rounds):
                        kind0, expert0, kind1, expert1 = (pe.snap(reg, min_val=0, max_val=hi) for reg, hi in zip(
                            carried, (KINDS_FULL + 3 * (U - 1), NE - 1) * 2))
                        this, after = (kind0, expert0), (kind1, expert1)
                        for u in range(U):
                            kind, expert = this
                            pe.wait_ge(hid2_ok, i * U + (u + 1))
                            gate_up(*after, (u + 1) % U, i * U + (u + 2))
                            this = after
                            after = of_block(i * U + (u + 2))
                            with pe.If(kind > KINDS_FULL - 1):
                                nc.tensor.transpose(PS[:, 4, 0:P], HB[:, u, 0:P], ident).then_inc(h2T_full, 1)
                            with pe.Else():
                                for c in range(2):
                                    last = nc.tensor.transpose(PS[:, 4, c * P:(c + 1) * P], HB[:, u, c * P:(c + 1) * P], ident)
                                last.then_inc(h2T_full, 1)
                            transpose_x((u + 2) % U, i * 16 + (32 if u else 16))
                            pe.wait_ge(down_arrived, expert + 1)
                            pe.wait_ge(y_act, i * U + (u + 1))
                            with pe.If(kind > KINDS_FULL - 1):
                                pe.wait_ge(h2T_out, i * U + (u + 1))
                                by_slot(kind, down_small, u)
                            with pe.Else():
                                pe.wait_ge(h2T_out, i * U + (u + 1))
                                slot = nc.s_assert_within(kind, 0, 3 * (U - 1))
                                for half in range(2):
                                    for c in range(2):
                                        last = nc.tensor.matmul(PS[:, 6 + half, :], HBT[:, u, c * P:(c + 1) * P],
                                                                WSLOT[:, bass.ds(slot + 2, 1), c * 1024 + half * 512:c * 1024 + (half + 1) * 512],
                                                                start=c == 0, stop=c == 1)
                                last.then_inc(y_full, 1)
                            slots((u + 1) % U, i * U + (u + 5))
                        carry()
        if upto == 4:
            return

        YL = ring(0, TL * D).rearrange("p (t n) -> p t n", t=TL)
        TB2 = pr(0, 2 * D).rearrange("p (b n) -> p b n", b=2)
        RF = pr(2 * D, 2 * TL).rearrange("p (t n) -> p t n", n=2)
        yl_ld = [sem(f"yl_ld{i}") for i in range(TL)]
        fin_sq, fin_sd, fin_ok, out_st = (sem(n) for n in ("fin_sq", "fin_sd", "fin_ok", "out_st"))
        with nc.Block() as block:
            @block.sync
            def _(sp):
                for i in range(TL):
                    sp.dma_start(YL[:, i], y_dram[i * P:(i + 1) * P, :]).then_inc(yl_ld[i], 16)
                for i in range(TL):
                    sp.wait_ge(fin_ok, i + 1)
                    sp.dma_start(out[0, i * P:(i + 1) * P, :], X[:, i]).then_inc(out_st, 16)
                sp.wait_ge(out_st, 16 * TL)

            @block.scalar
            def _(act):
                for i in range(TL):
                    act.wait_ge(yl_ld[i], 16)
                    if i >= 2:
                        act.wait_ge(fin_ok, i - 1)
                    nc.scalar.activation(TB2[:, i % 2], YL[:, i], ACT.Square, accum_out=RF[:, i, 0:1]).then_inc(fin_sq, 1)
                    act.wait_ge(fin_sq, i + 1)
                    nc.scalar.activation(RF[:, i, 1:2], RF[:, i, 0:1], ACT.Sqrt, bias=const("eps"), scale=1.0 / D).then_inc(fin_sd, 1)

            @block.vector
            def _(dve):
                for i in range(TL):
                    dve.wait_ge(fin_sd, i + 1)
                    own(dve, dve_own, dve_n, nc.vector.reciprocal(RF[:, i, 1:2], RF[:, i, 1:2]))
                    own(dve, dve_own, dve_n, nc.vector.scalar_tensor_tensor(out=TB2[:, i % 2], in0=YL[:, i], scalar=RF[:, i, 1:2], in1=BC[:, 3],
                                                                            op0=ALU.mult, op1=ALU.mult))
                    nc.vector.tensor_tensor(X[:, i], X[:, i], TB2[:, i % 2], ALU.add).then_inc(fin_ok, 1)


NAMES = ["x", "c", "ctx", "c_ctx", "w_mod", "b_mod", "norm_g", "w_in", "ret_log_decay", "ret_norm_g", "mlstm_conv_w",
         "mlstm_conv_b", "mlstm_gate_b", "mlstm_norm_g", "w_out", "w_router", "router_bias", "w_gate", "w_up", "w_down",
         "ws_gate", "ws_up", "ws_down"]


def kernel(**inputs):
    import numpy as _np
    import concourse.bacc as _bacc
    from concourse import mybir as _mybir
    from concourse.bass_utils import run_bass_kernel_spmd as _run

    nc = _bacc.Bacc("TRN2", target_bir_lowering=False, num_devices=1)
    arrays, args = {}, {}
    for name in NAMES + ["consts"]:
        a = constants() if name == "consts" else _np.ascontiguousarray(inputs[name])
        arrays[f"in_{name}"] = a
        args[name] = nc.dram_tensor(f"in_{name}", a.shape, _mybir.dt.from_np(a.dtype), kind="ExternalInput").ap()
    out = nc.dram_tensor("out_0", (1, SEQ, D), F32, kind="ExternalOutput").ap()
    build(nc, args, out)
    r = _run(nc, [arrays], core_ids=[0])
    return r.results[0]["out_0"]
```
